# Optimizing a Trainium2 kernel written in Bass

```python
import jax, jax.numpy as jnp
from jax import lax
import numpy as np

D_MODEL = 1024
BATCH = 1
SEQ = 256
DEPTH = 1
DEC_BATCH = 8
DEC_SEQ = 1
PAST_LEN = 1024
PAGE_SIZE = 128

N_HEADS = 16
HEAD_DIM = 64
ATTN_WIDTH = N_HEADS * HEAD_DIM
CONV_CH = 1024
CONV_WIDTH = 31
N_EXPERTS = 32
TOP_K = 4
D_FF = 1024
SWIGLU_ALPHA = 1.702
SWIGLU_LIMIT = 7.0
Q_BLOCK = 128
LN_EPS = 1e-5
DEEPNORM_ALPHA = (2 * DEPTH) ** 0.25
DEEPNORM_BETA = (8 * DEPTH) ** -0.25
D_IN_PROJ = 3 * ATTN_WIDTH + N_HEADS + 2 * CONV_CH + 2 * D_MODEL

kernel_name = "fox_conformer_gated_moe_step"

def layer_norm(x, g, b):
    xf = x.astype(jnp.float32)
    mu = jnp.mean(xf, axis=-1, keepdims=True)
    var = jnp.mean(jnp.square(xf - mu), axis=-1, keepdims=True)
    y = (xf - mu) * lax.rsqrt(var + LN_EPS) * g.astype(jnp.float32) + b.astype(jnp.float32)
    return y.astype(x.dtype)

def in_projection(h, w_in, b_forget):
    N, L, _ = h.shape
    sizes = [ATTN_WIDTH, ATTN_WIDTH, ATTN_WIDTH, N_HEADS, CONV_CH, CONV_CH, D_MODEL]
    points = [int(p) for p in np.cumsum(sizes)]
    proj = h @ w_in
    q, k, v, f, u_val, u_gate, g_attn, g_conv = jnp.split(proj, points, axis=-1)
    q = q.reshape(N, L, N_HEADS, HEAD_DIM)
    k = k.reshape(N, L, N_HEADS, HEAD_DIM)
    v = v.reshape(N, L, N_HEADS, HEAD_DIM)
    logf = jax.nn.log_sigmoid(f.astype(jnp.float32) + b_forget.astype(jnp.float32))
    u = u_val * jax.nn.sigmoid(u_gate)
    return q, k, v, logf, u, g_attn, g_conv

def forgetting_attention_prompt(q, k, v, logf):
    B, S = q.shape[0], q.shape[1]
    n_blk = S // Q_BLOCK
    scale = HEAD_DIM ** -0.5
    c = jnp.cumsum(logf, axis=1)
    c_keys = jnp.transpose(c, (0, 2, 1))
    k_pos = jnp.arange(S)

    def one_block(args):
        q_blk, c_blk, q_pos = args
        s = jnp.einsum('bqhd,bkhd->bhqk', q_blk, k).astype(jnp.float32) * scale
        bias = jnp.transpose(c_blk, (0, 2, 1))[..., None] - c_keys[:, :, None, :]
        mask = k_pos[None, :] <= q_pos[:, None]
        p = jax.nn.softmax(jnp.where(mask, s + bias, -jnp.inf), axis=-1).astype(v.dtype)
        return jnp.einsum('bhqk,bkhd->bqhd', p, v)

    q_blocks = q.reshape(B, n_blk, Q_BLOCK, N_HEADS, HEAD_DIM).transpose(1, 0, 2, 3, 4)
    c_blocks = c.reshape(B, n_blk, Q_BLOCK, N_HEADS).transpose(1, 0, 2, 3)
    pos_blocks = jnp.arange(S).reshape(n_blk, Q_BLOCK)
    out = lax.map(one_block, (q_blocks, c_blocks, pos_blocks))
    return out.transpose(1, 0, 2, 3, 4).reshape(B, S, N_HEADS, HEAD_DIM)

def forgetting_attention_sample(q, k_new, v_new, logf_new, cache_k, cache_v, cache_logf, page_table):
    DB, DS = q.shape[0], q.shape[1]
    past = page_table.shape[1] * PAGE_SIZE
    scale = HEAD_DIM ** -0.5
    k_past = cache_k[page_table].reshape(DB, past, N_HEADS, HEAD_DIM)
    v_past = cache_v[page_table].reshape(DB, past, N_HEADS, HEAD_DIM)
    lf_past = cache_logf[page_table].reshape(DB, past, N_HEADS).astype(jnp.float32)
    k_all = jnp.concatenate([k_past, k_new.astype(k_past.dtype)], axis=1)
    v_all = jnp.concatenate([v_past, v_new.astype(v_past.dtype)], axis=1)
    lf_all = jnp.concatenate([lf_past, logf_new], axis=1)
    after = lax.cumsum(lf_all, axis=1, reverse=True) - lf_all
    after_k = jnp.transpose(after, (0, 2, 1))
    bias = after_k[:, :, None, :] - after_k[:, :, past:, None]
    s = jnp.einsum('bqhd,bkhd->bhqk', q, k_all).astype(jnp.float32) * scale + bias
    q_pos = past + jnp.arange(DS)
    k_pos = jnp.arange(past + DS)
    mask = k_pos[None, :] <= q_pos[:, None]
    p = jax.nn.softmax(jnp.where(mask, s, -jnp.inf), axis=-1).astype(v_all.dtype)
    return jnp.einsum('bhqk,bkhd->bqhd', p, v_all)

def causal_depthwise_conv(u, prev, conv_w, conv_b):
    full = jnp.concatenate([prev.astype(u.dtype), u], axis=1)
    y = lax.conv_general_dilated(full, conv_w[:, None, :].astype(u.dtype), window_strides=(1,),
                                 padding='VALID', dimension_numbers=('NWC', 'WIO', 'NWC'),
                                 feature_group_count=CONV_CH)
    return y + conv_b, full[:, -(CONV_WIDTH - 1):]

def conv_branch(u, prev, conv_w, conv_b, conv_norm_g, conv_norm_b):
    y, new_prev = causal_depthwise_conv(u, prev, conv_w, conv_b)
    y = layer_norm(y, conv_norm_g, conv_norm_b)
    return jax.nn.silu(y), new_prev

def merge_branches(att, conv, g_attn, g_conv, w_attn_proj, w_conv_proj, w_out):
    N, L = att.shape[0], att.shape[1]
    a = att.reshape(N, L, ATTN_WIDTH) @ w_attn_proj
    c = conv @ w_conv_proj
    return (jax.nn.sigmoid(g_attn) * a + jax.nn.sigmoid(g_conv) * c) @ w_out

def routed_experts(x, w_router, b_router, w_gate_up, b_gate_up, w_down, b_down):
    logits = (x @ w_router).astype(jnp.float32) + b_router.astype(jnp.float32)
    top_logits, top_idx = lax.top_k(logits, TOP_K)
    top_w = jax.nn.softmax(top_logits, axis=-1)
    combine = jnp.einsum('tk,tke->te', top_w,
                         jax.nn.one_hot(top_idx, N_EXPERTS, dtype=jnp.float32)).astype(x.dtype)
    out = jnp.zeros_like(x)
    for e in range(N_EXPERTS):
        gu = x @ w_gate_up[e] + b_gate_up[e]
        gate = jnp.minimum(gu[:, :D_FF], SWIGLU_LIMIT)
        up = jnp.clip(gu[:, D_FF:], -SWIGLU_LIMIT, SWIGLU_LIMIT)
        act = (up + 1.0) * gate * jax.nn.sigmoid(SWIGLU_ALPHA * gate)
        out = out + combine[:, e:e + 1] * (act @ w_down[e] + b_down[e])
    return out

def trunk_layer(xp, xs, cache_k, cache_v, cache_logf, state_conv, page_table,
                w_in, b_forget, conv_w, conv_b, conv_norm_g, conv_norm_b,
                w_attn_proj, w_conv_proj, w_out, ln1_g, ln1_b,
                w_router, b_router, w_gate_up, b_gate_up, w_down, b_down, ln2_g, ln2_b):
    B, S, D = xp.shape
    DB, DS, _ = xs.shape
    qp, kp, vp, lfp, up, gap, gcp = in_projection(xp, w_in, b_forget)
    att_p = forgetting_attention_prompt(qp, kp, vp, lfp)
    conv_p, conv_state_p = conv_branch(up, jnp.zeros((B, CONV_WIDTH - 1, CONV_CH), up.dtype),
                                       conv_w, conv_b, conv_norm_g, conv_norm_b)
    mix_p = merge_branches(att_p, conv_p, gap, gcp, w_attn_proj, w_conv_proj, w_out)
    qs, ks, vs, lfs, us, gas, gcs = in_projection(xs, w_in, b_forget)
    att_s = forgetting_attention_sample(qs, ks, vs, lfs, cache_k, cache_v, cache_logf, page_table)
    conv_s, conv_state_s = conv_branch(us, state_conv, conv_w, conv_b, conv_norm_g, conv_norm_b)
    mix_s = merge_branches(att_s, conv_s, gas, gcs, w_attn_proj, w_conv_proj, w_out)
    res = jnp.concatenate([(DEEPNORM_ALPHA * xp + mix_p).reshape(B * S, D),
                           (DEEPNORM_ALPHA * xs + mix_s).reshape(DB * DS, D)], axis=0)
    h = layer_norm(res, ln1_g, ln1_b)
    h = layer_norm(DEEPNORM_ALPHA * h + routed_experts(h, w_router, b_router, w_gate_up,
                                                        b_gate_up, w_down, b_down), ln2_g, ln2_b)
    y_p = h[:B * S].reshape(B, S, D)
    y_s = h[B * S:].reshape(DB, DS, D)
    return (y_p, y_s, kp, vp, lfp, conv_state_p, ks, vs, lfs, conv_state_s)

def setup_inputs(seed: int = 0) -> dict:
    key = jax.random.key(seed)
    ks = jax.random.split(key, 32)
    f32 = jnp.float32
    n_pages = PAST_LEN // PAGE_SIZE
    n_phys = (5 * DEC_BATCH * n_pages + 3) // 4

    def normal(k, shape, scale=1.0):
        return jax.random.normal(k, shape, f32) * scale

    x_prompt = normal(ks[0], (BATCH, SEQ, D_MODEL))
    x_sample = normal(ks[1], (DEC_BATCH, DEC_SEQ, D_MODEL))
    cache_k = normal(ks[2], (DEPTH, n_phys, PAGE_SIZE, N_HEADS, HEAD_DIM))
    cache_v = normal(ks[3], (DEPTH, n_phys, PAGE_SIZE, N_HEADS, HEAD_DIM))
    cache_logf = jax.nn.log_sigmoid(
        jax.random.uniform(ks[4], (DEPTH, 1, 1, N_HEADS), f32, 1.0, 6.0)
        + normal(ks[5], (DEPTH, n_phys, PAGE_SIZE, N_HEADS)))
    state_conv = normal(ks[6], (DEPTH, DEC_BATCH, CONV_WIDTH - 1, CONV_CH), 0.5)
    page_table = jax.random.permutation(ks[7], n_phys)[:DEC_BATCH * n_pages].reshape(
        DEC_BATCH, n_pages).astype(jnp.int32)
    return {
        "x_prompt": x_prompt,
        "x_sample": x_sample,
        "cache_k": cache_k,
        "cache_v": cache_v,
        "cache_logf": cache_logf,
        "state_conv": state_conv,
        "page_table": page_table,
        "w_in": normal(ks[8], (DEPTH, D_MODEL, D_IN_PROJ), D_MODEL ** -0.5),
        "b_forget": jax.random.uniform(ks[9], (DEPTH, N_HEADS), f32, 1.0, 6.0),
        "conv_w": normal(ks[10], (DEPTH, CONV_WIDTH, CONV_CH), CONV_WIDTH ** -0.5),
        "conv_b": normal(ks[11], (DEPTH, CONV_CH), 0.02),
        "conv_norm_g": 1.0 + normal(ks[12], (DEPTH, CONV_CH), 0.02),
        "conv_norm_b": normal(ks[13], (DEPTH, CONV_CH), 0.02),
        "w_attn_proj": normal(ks[14], (DEPTH, ATTN_WIDTH, D_MODEL), ATTN_WIDTH ** -0.5),
        "w_conv_proj": normal(ks[15], (DEPTH, CONV_CH, D_MODEL), CONV_CH ** -0.5),
        "w_out": normal(ks[16], (DEPTH, D_MODEL, D_MODEL), D_MODEL ** -0.5 * DEEPNORM_BETA),
        "ln1_g": 1.0 + normal(ks[17], (DEPTH, D_MODEL), 0.02),
        "ln1_b": normal(ks[18], (DEPTH, D_MODEL), 0.02),
        "w_router": normal(ks[19], (DEPTH, D_MODEL, N_EXPERTS), D_MODEL ** -0.5),
        "b_router": normal(ks[20], (DEPTH, N_EXPERTS), 0.01),
        "w_gate_up": normal(ks[21], (DEPTH, N_EXPERTS, D_MODEL, 2 * D_FF), D_MODEL ** -0.5),
        "b_gate_up": normal(ks[22], (DEPTH, N_EXPERTS, 2 * D_FF), 0.02),
        "w_down": normal(ks[23], (DEPTH, N_EXPERTS, D_FF, D_MODEL), D_FF ** -0.5 * DEEPNORM_BETA),
        "b_down": normal(ks[24], (DEPTH, N_EXPERTS, D_MODEL), 0.02),
        "ln2_g": 1.0 + normal(ks[25], (DEPTH, D_MODEL), 0.02),
        "ln2_b": normal(ks[26], (DEPTH, D_MODEL), 0.02),
    }

def reference(x_prompt, x_sample, cache_k, cache_v, cache_logf, state_conv, page_table,
              w_in, b_forget, conv_w, conv_b, conv_norm_g, conv_norm_b,
              w_attn_proj, w_conv_proj, w_out, ln1_g, ln1_b,
              w_router, b_router, w_gate_up, b_gate_up, w_down, b_down, ln2_g, ln2_b):
    xp, xs = x_prompt, x_sample
    rows = []
    for layer in range(DEPTH):
        out = trunk_layer(xp, xs, cache_k[layer], cache_v[layer], cache_logf[layer],
                          state_conv[layer], page_table,
                          w_in[layer], b_forget[layer], conv_w[layer], conv_b[layer],
                          conv_norm_g[layer], conv_norm_b[layer], w_attn_proj[layer],
                          w_conv_proj[layer], w_out[layer], ln1_g[layer], ln1_b[layer],
                          w_router[layer], b_router[layer], w_gate_up[layer], b_gate_up[layer],
                          w_down[layer], b_down[layer], ln2_g[layer], ln2_b[layer])
        xp, xs = out[0], out[1]
        rows.append(out[2:])
    k_prompt = jnp.stack([r[0] for r in rows])
    v_prompt = jnp.stack([r[1] for r in rows])
    logf_prompt = jnp.stack([r[2] for r in rows])
    conv_prompt = jnp.stack([r[3] for r in rows])
    k_sample = jnp.stack([r[4] for r in rows])
    v_sample = jnp.stack([r[5] for r in rows])
    logf_sample = jnp.stack([r[6] for r in rows])
    conv_sample = jnp.stack([r[7] for r in rows])
    return (xp, xs, k_prompt, v_prompt, logf_prompt, conv_prompt,
            k_sample, v_sample, logf_sample, conv_sample)


_drawn_inputs = setup_inputs


def setup_inputs(seed=0):
    import zlib

    import numpy as np

    out = dict(_drawn_inputs(seed))
    spreads = {}
    factors = {'conv_b': 3.503,
     'conv_norm_g': 5.571,
     'conv_norm_b': 5.881,
     'b_gate_up': 8.0,
     'b_down': 6.324,
     'ln2_g': 7.949,
     'ln2_b': 7.862,
     'b_router': 3.06}
    for name, (base, spread) in spreads.items():
        noise = np.random.default_rng([zlib.crc32(name.encode()), seed]).standard_normal(out[name].shape)
        drawn = base * np.exp(spread * noise) if base else spread * noise
        out[name] = __import__('jax').numpy.asarray(drawn.astype(out[name].dtype))
    for name, factor in factors.items():
        out[name] = (out[name] * factor).astype(out[name].dtype)
    return out
```

```python
from contextlib import ExitStack

import concourse.bass as bass
from concourse import mybir

F32 = mybir.dt.float32
F32R = mybir.dt.float32r
I32 = mybir.dt.int32
ALU = mybir.AluOpType
ACT = mybir.ActivationFunctionType
X = mybir.AxisListType.X

P = 128
NEG = -1.0e30
LIMIT = 7.0
SWIGLU_ALPHA = 1.702
EPS = 1e-5
TOP_K = 4
ALPHA = 2.0 ** 0.25
CAP = 64
POOL_SPLITS = (3, 6, 9)
POOL_PAGES = (1, 3, 5, 7)

SEMAPHORES = """
x_loaded params_loaded table_loaded forget_loaded lf_loaded logf_new_loaded late_loaded xres_loaded
ln1_loaded ln2_loaded bdown_loaded extras_loaded extras_stored pool_consts x_turned x_copied
params_turned params_copied smp_products smp_conv_mm logit_mm neg_abs softplus logf_done logf_stored
proj_done proj_used q_turned q_copied q_stored qb_free kv_turned kv_copied kv_stored prodP_full
prodP_free scores_done self_done after_sums bias_mm max_part max_turned max_diag max_spread shifted
sample_exps sum_part sum_spread u_sig conv_done uout_turned uout_copied conv_stored staged
prompt_read scores_mm row_max exps probs_done turned_mm probsT_copied oT_copied v_mm att_done
smp_out own_masked own_turned mean_mm centred squares var_mm var_done std_done normed conv_act gates
gated mixT_copied mix_turned resid row_var row_std h_done h_turned hT_copied router_mm logits_max
exps_r mask_done rank_mm weights_done wT_turned wT_copied bdown_mm acc_init extras_made items_ready
b_turned b_copied h_hi_done h_lo_done sel_ready selw_ready gather_mm rows_copied tokens_turned
xg_ready gu_copied gu_turned gate_ready sigmoid_done act_ready selw_turned selT_copied scatter_mm
scatter_added out_copied y_turned y_done y_stored
""".split()


def trunk_step(nc, x_prompt, x_sample, cache_k, cache_v, cache_logf, state_conv, page_table,
               w_in, b_forget, conv_w, conv_b, conv_norm_g, conv_norm_b,
               w_attn_proj, w_conv_proj, w_out, ln1_g, ln1_b,
               w_router, b_router, w_gate_up, b_gate_up, w_down, b_down, ln2_g, ln2_b,
               y_prompt, y_sample, k_prompt, v_prompt, logf_prompt, conv_prompt,
               k_sample, v_sample, logf_sample, conv_sample):
    _, SEQ, D = x_prompt.shape
    NS = x_sample.shape[0]
    _, _, PAGE, H, HD = cache_k.shape
    NPG = page_table.shape[1]
    W = conv_w.shape[1]
    E = w_router.shape[2]
    FF = w_down.shape[2]
    KT = D // P
    TOK = SEQ + NS
    TILES = [(0, P), (P, P), (2 * P, NS)]
    NT = len(TILES)
    SH = NS * H
    SCALE = float(HD) ** -0.5
    SEC = 7
    CH = KT * TOK
    N_EXTRA = TOK * TOP_K // CAP
    LIST = 64
    assert SEQ == 2 * P and D == 1024 and FF == D and PAGE == P and H * HD == D and NS == 8 and NPG == 8
    assert E + N_EXTRA + 2 < LIST and CAP * 4 <= TOK <= CAP * 5

    q_scratch = nc.dram_tensor("q_scratch", [NS, D], F32, kind="Internal").ap()
    extras_scratch = nc.dram_tensor("extras_scratch", [N_EXTRA + 2, 2], I32, kind="Internal").ap()
    kpages = cache_k.rearrange("o n p h d -> (o n) p (h d)")
    vpages = cache_v.rearrange("o n p h d -> (o n) p (h d)")
    fpages = cache_logf.rearrange("o n p h -> (o n) p h")
    x_rows = [x_prompt[0, 0:P, :], x_prompt[0, P:SEQ, :], x_sample.rearrange("b s d -> (b s) d")]
    y_rows = [y_prompt[0, 0:P, :], y_prompt[0, P:SEQ, :], y_sample.rearrange("b s d -> (b s) d")]
    kp_rows, vp_rows = (a.rearrange("o b s h d -> (o b s) (h d)") for a in (k_prompt, v_prompt))
    ks_rows, vs_rows = (a.rearrange("o b s h d -> (o b s) (h d)") for a in (k_sample, v_sample))
    k_rows = [kp_rows[0:P, :], kp_rows[P:SEQ, :], ks_rows]
    v_rows = [vp_rows[0:P, :], vp_rows[P:SEQ, :], vs_rows]
    lfp_rows = logf_prompt.rearrange("o b (t p) h -> p (o b t) h", p=P)
    lfs_rows = logf_sample.rearrange("o b s h -> (o b s) h")
    w_in_v = w_in.rearrange("o (k p) n -> p (o k) n", p=P)
    proj_w = [w.rearrange("o (k p) n -> p (o k) n", p=P) for w in (w_attn_proj, w_conv_proj, w_out)]
    gu_v = w_gate_up.rearrange("o e (k p) n -> (o e) k p n", p=P)
    dn_v = w_down.rearrange("o e (k t p) n -> (o e) k p t n", p=P, t=2)

    def row(par):
        return par.rearrange("o n -> (o n)").partition_broadcast(P)

    with ExitStack() as ctx:
        def sb(name, shape, dt=F32):
            return ctx.enter_context(nc.sbuf_tensor(name, shape, dt))

        sem = {n: ctx.enter_context(nc.semaphore(n)) for n in SEMAPHORES}
        full = [ctx.enter_context(nc.semaphore(f"full{i}")) for i in range(12)]
        free = [ctx.enter_context(nc.semaphore(f"free{i}")) for i in range(12)]
        hi_done = [ctx.enter_context(nc.semaphore(f"hi_done{i}")) for i in range(3)]
        lo_done = [ctx.enter_context(nc.semaphore(f"lo_done{i}")) for i in range(3)]
        pair_free = [ctx.enter_context(nc.semaphore(f"pair_free{i}")) for i in range(3)]
        qb_full = [ctx.enter_context(nc.semaphore(f"qb_full{i}")) for i in range(2)]

        places = {}

        def placed(name, shape):
            places[name] = nc.sbuf_base
            return sb(name, shape)

        def parts_at(name, shape, tensor, col):
            return nc.alloc_sbuf_tensor_at(name, shape, F32R, offset=-(-places[tensor] // 32) * 32 + 4 * col)

        ring = placed("ring", [P, 12, 2048])
        proj = placed("proj", [P, SEC * CH])
        xT = sb("xT", [P, KT, TOK])
        v_nat = placed("v_nat", [P, NT, D])
        S_smp = sb("S_smp", [P, NPG + 1, SH])
        lf = placed("lf", [P, NPG, SH])
        lf_after = placed("lf_after", [P, NPG, SH])
        asc = sb("asc", [P, 3072])
        ident = sb("ident", [P, P])
        tri = sb("tri", [P, P])
        ones_after = sb("ones_after", [P, 2 * P])
        cmask = sb("cmask", [P, 3 * P])
        smask = sb("smask", [NS, NS, H])
        blk = sb("blk", [P, 4])
        cw = sb("cw", [P, KT, W])
        cpar = sb("cpar", [P, 3 * KT])
        wf = sb("wf", [P, KT, H])
        bf_row = sb("bf_row", [P, H])
        page_ids = sb("page_ids", [1, NS * NPG], I32)
        small = sb("small", [P, 448])
        items = sb("items", [1, LIST, 2], I32)
        extra_items = sb("extra_items", [P, 2], I32)
        n_extra_i = sb("n_extra_i", [1, 2], I32)

        def sec(s):
            return proj[:, s * CH:(s + 1) * CH].rearrange("p (k t) -> p k t", t=TOK)

        qT, kT, vT, u_val, u_gate, g_att, g_conv = (sec(s) for s in range(SEC))
        y_conv = u_gate
        squares = u_val
        early = ring[:, 8:12, :].rearrange("p a n -> p (a n)")
        qb = [early[:, i * D:(i + 1) * D] for i in range(2)]
        prodD = [early[:, 2 * D:3 * D], asc[:, 0:D]]
        prodP = [early[:, (3 + i) * D:(4 + i) * D] for i in range(2)]
        x_nat = early[:, 5 * D:8 * D].rearrange("p (t d) -> p t d", d=D)
        k_nat = x_nat
        SR = 4 * (W - 1)
        state_nat = v_nat[0:SR, 0:2, :]
        cw_rows = v_nat[0:SR, 2, :]
        convw_nat = asc[0:W, 0:D]
        cpar_nat = asc[0:3 * KT, D:D + P]
        self_prod = asc[0:NS, 0:D]
        q_nat = asc[0:NS, 1280:1280 + D]
        lf_cols, la_cols = (a[:, :, :].rearrange("p g n -> p (g n)") for a in (lf, lf_after))
        q_st = [asc[:, 0:256], lf_cols[:, 0:256]]
        k_st = [asc[:, 256:512], lf_cols[:, 256:512]]
        v_st = [a.rearrange("p (t c) -> p t c", c=P) for a in (asc[:, 512:768], lf_cols[:, 512:768])]
        decay = [a.rearrange("p (h a c) -> p h a c", h=2, c=P) for a in (asc[:, 768:1536], la_cols[:, 0:768])]
        p_st = [a[:, 768:768 + (NPG + 1) * H].rearrange("p (g h) -> p g h", h=H) for a in (lf_cols, la_cols)]
        probs = asc[:, 1536:2304].rearrange("p (h c) -> p h c", h=2)
        probsT = asc[:, 2304:3072].rearrange("p (h c) -> p h c", h=2)
        attT = xT
        own_heads = proj[0:H, 2 * CH:2 * CH + D]
        LATE = (W + 1) // 2
        late_sums = [proj[:, 2 * CH + D + a * SEQ:2 * CH + D + a * SEQ + SEQ - LATE] for a in range(2)]
        h_nat = proj[:, 0:3 * D].rearrange("p (t d) -> p t d", d=D)
        ln_g, ln_b = proj[:, 3 * D:4 * D], proj[:, 4 * D:5 * D]
        out_sb = proj[:, 5 * D:6 * D]
        mixT, hT, mT, accT = u_val, u_gate, g_conv, xT
        m0, m1 = 3 * CH, 4 * CH
        g_buf, u_buf, s_buf, act_buf = (
            proj[:, m0 + 512 * i:m0 + 512 * (i + 1)].rearrange("p (k s) -> p k s", s=CAP) for i in range(4))
        gu_sb = proj[:, m1:m1 + 2 * FF]
        selT = lf_cols[:, 0:TOK]
        selw = lf_cols[:, TOK:TOK + 2 * NT * CAP].rearrange("p (t s) -> p t s", s=2 * CAP)
        x_rows_r = parts_at("x_rows_r", [P, D], "proj", 0)
        sel = parts_at("sel", [P, NT, 3 * CAP], "proj", D)
        ident_r = parts_at("ident_r", [P, P], "proj", D + 9 * CAP)
        act2 = parts_at("act2", [P, KT, 2 * CAP], "lf_after", 0)
        h_hi = parts_at("h_hi", [P, NT, D], "v_nat", 0)
        h_lo = parts_at("h_lo", [P, NT, D], "proj", 5 * CH)
        xg = parts_at("xg", [P, KT, 2 * CAP], "proj", 5 * CH + 3 * D)
        w_hi = [parts_at(f"w_hi{i}", [P, 2048], "ring", 2048 * (10, 0, 2)[i]) for i in range(3)]
        w_lo = [parts_at(f"w_lo{i}", [P, 2048], "ring", 2048 * (11, 1, 3)[i]) for i in range(3)]
        y_nat = proj[:, 5 * CH:5 * CH + 3 * D].rearrange("p (t d) -> p t d", d=D)
        bd_nat = S_smp[0:E, 0:NPG, :].rearrange("p g n -> p (g n)")
        uout_p, uout_s = (a.rearrange("p g n -> p (g n)") for a in (lf[0:W - 1], lf_after[0:NS]))
        rt = asc[:, 0:904]
        logits, above, ties, mask, wts, slot = (
            rt[:, 96 * i:96 * (i + 1)].rearrange("p (t e) -> p t e", e=E) for i in range(6))
        top8 = rt[:, 576:600].rearrange("p (t e) -> p t e", e=8)
        n_above, wsum, nbig = rt[:, 600:603], rt[:, 603:606], rt[:, 606:609]
        counts = rt[:, 609:641]
        flags, prefix = rt[:, 641:769], rt[:, 769:897]
        eidx = rt[:, 897:903]
        iota_f = asc[:, 904:1288]
        wcT = asc[0:E, 1288:1288 + TOK]
        tri_s = asc[:, 1552:1680]
        router_w = asc[:, 1680:1936].rearrange("p (k e) -> p k e", e=E)
        bgu_nat = asc[:, 1936:2448].rearrange("p (a b) -> p a b", b=P)
        bias_gu = asc[:, 2448:2960]
        br_row = asc[:, 2960:2992]
        sum_halves = asc[:, 2992:3056]
        zf, na, logf = (small[:, 48 * i:48 * (i + 1)].rearrange("p (t h) -> p t h", h=H) for i in range(3))
        self_s = small[0:NS, 144:160]
        nmax = small[:, 160:164].rearrange("p (h a) -> p h a", h=2)
        psums = small[:, 164:168].rearrange("p (h a) -> p h a", h=2)
        smax = small[:, 168:169]
        lnst = small[:, 170:182].rearrange("p (a b) -> p a b", b=6)
        mv, rstd = small[:, 182:184], small[:, 184:185]
        kidx = small[:, 186:187]
        smp_conv = small[:, 192:256].rearrange("p (c b) -> p c b", b=NS)
        part = small[:, 256:384]
        logf_row = sb("logf_row", [1, SH])

        onesm, after = ones_after[:, 0:P], ones_after[:, P:2 * P]
        pb = [ctx.enter_context(nc.psum_tensor(f"pb{i}", [P, 512], F32)) for i in range(8)]
        block = ctx.enter_context(nc.Block())

        def bank(i, k):
            return pb[i][:, :].rearrange("p (k n) -> p k n", k=k)

        Q0_USES, K_USES, V_USES = SEC + 3, NS, NS // 2

        PLACES, SLOTS = 12, 6

        def slot_of(place):
            return (place + 2) % SLOTS

        def pair_of(place):
            return (place + 2) % 3

        def loaded(place, i):
            s = slot_of(place)
            before = 32 * (K_USES + V_USES) if s < 4 else 32 * V_USES
            return i * 32 + (before + 16 * ((place - 4) // SLOTS + 1))

        def split(place, i):
            return i * 4 + ((place - 4) // 3 + 1)

        def used(place, i):
            return split(place, i) + 1

        @block.sync
        def _(sp):
            def load_w(src, use, c):
                sp.wait_ge(free[c], use + 1)
                sp.dma_start(ring[:, c, :].rearrange("p (k n) -> p k n", k=KT), src).then_inc(full[c], 16)

            def w_in_cols(start, c):
                return w_in_v[:, :, bass.ds(start + 256 * c, 256)]

            def load_pages(pages, s, r, buf, uses):
                sp.wait_ge(free[buf], uses + 1)
                for g in (2 * r, 2 * r + 1):
                    pid = sp.value_load(page_ids[0:1, bass.ds(s * NPG + g, 1)], min_val=0,
                                        max_val=cache_k.shape[1] - 1)
                    sp.dma_start(ring[:, buf, (g % 2) * D:(g % 2 + 1) * D],
                                 pages[bass.ds(pid, 1), :, :].rearrange("o p n -> (o p) n"))\
                        .then_inc(full[buf], 16)
                    if pages is kpages:
                        sp.dma_start(lf[:, g, bass.ds(s * H, H)],
                                     fpages[bass.ds(pid, 1), :, :].rearrange("o p n -> (o p) n"))\
                            .then_inc(sem["lf_loaded"], 16)

            def load_query(s, par):
                sp.wait_ge(sem["qb_free"], s + 1)
                sp.dma_start(qb[par], q_scratch[bass.ds(s, 1), :].rearrange("o n -> (o n)")
                             .partition_broadcast(P)).then_inc(qb_full[par], 16)

            for b in range(12):
                sp.sem_inc(free[b], 1)
            for t, (r0, n) in enumerate(TILES):
                sp.dma_start(x_nat[0:n, t, :], x_rows[t]).then_inc(sem["x_loaded"], 16)
            load_w(w_in_cols(0, 0), 0, 0)
            sp.dma_start(page_ids[:, :], page_table.rearrange("a (o b) -> o (a b)", o=1))\
                .then_inc(sem["table_loaded"], 16)
            for c in range(1, 4):
                load_w(w_in_cols(0, c), 0, c)
            sp.dma_start(wf[:, :, :], w_in_v[:, :, 3 * D:3 * D + H]).then_inc(sem["forget_loaded"], 16)
            sp.dma_start(bf_row[:, :], row(b_forget)).then_inc(sem["forget_loaded"], 16)
            sp.dma_start(convw_nat, conv_w[0, :, :]).then_inc(sem["params_loaded"], 16)
            for i, par in enumerate((conv_b, conv_norm_g, conv_norm_b)):
                sp.dma_start(cpar_nat[i * KT:(i + 1) * KT, :], par.rearrange("o (k p) -> (o k) p", p=P))\
                    .then_inc(sem["params_loaded"], 16)
            for i in range(2):
                sp.dma_start(state_nat[:, i, :],
                             state_conv[0, 4 * i:4 * i + 4, :, :].rearrange("b w c -> (b w) c"))\
                    .then_inc(sem["params_loaded"], 16)
            for i in range(4):
                sp.dma_start(cw_rows[i * (W - 1):(i + 1) * (W - 1), :], conv_w[0, 0:W - 1, :])\
                    .then_inc(sem["params_loaded"], 16)
            sp.wait_ge(sem["table_loaded"], 16)
            for r in range(4):
                load_pages(kpages, 0, r, 4 + r, 0)
            for c in range(4):
                load_w(w_in_cols(D, c), 1, c)
            sp.wait_ge(sem["q_stored"], 16)
            load_query(0, 0)

            def keys_and_section(s, start, use):
                for c in range(4):
                    if c % 2 == 0:
                        load_query(s + c // 2, 1 - c // 2)
                    for r in (2 * c % 4, 2 * c % 4 + 1):
                        load_pages(kpages, s + c // 2, r, 4 + r, s + c // 2)
                    load_w(w_in_cols(start, c), use, c)

            keys_and_section(1, 2 * D, 2)
            with sp.Fori(0, 2) as i:
                keys_and_section(i * 2 + 3, i * D + (3 * D + H), i + 3)
            load_query(NS - 1, 1)
            for r in range(4):
                load_pages(kpages, NS - 1, r, 4 + r, NS - 1)
                load_w(w_in_cols(5 * D + H, r), 5, r)
            for c in range(4):
                load_w(w_in_cols(6 * D + H, c), 6, c)
            sp.wait_ge(sem["logf_stored"], 32)
            sp.dma_start(logf_row[:, :], lfs_rows.rearrange("s (o h) -> o s h", o=1))\
                .then_inc(sem["logf_new_loaded"], 16)
            sp.dma_start(conv_sample[0, :, 0:W - 2, :], state_conv[0, :, 1:W - 1, :])\
                .then_inc(sem["conv_stored"], 16)
            for r in range(4):
                load_pages(vpages, 0, r, 4 + r, K_USES)
            sp.wait_ge(sem["scores_done"], NS)
            sp.wait_ge(sem["self_done"], 1)
            sp.wait_ge(sem["kv_stored"], 16 * 2 * NT)
            for r in range(4):
                load_pages(vpages, 1, r, 8 + r, 0)
            for c in range(4):
                load_w(proj_w[0][:, :, 256 * c:256 * (c + 1)], SEC, c)
            with sp.Fori(1, NS // 2) as i:
                for par in range(2):
                    for r in range(4):
                        load_pages(vpages, i * 2 + par, r, 4 + 4 * par + r,
                                   i + K_USES if par == 0 else i)

            def load_chunk(src, place, i, first=False):
                s = slot_of(place)
                if first:
                    sp.wait_ge(free[4 + s], (K_USES + V_USES if s < 4 else V_USES) + 1)
                else:
                    sp.wait_ge(lo_done[pair_of(place)], split(place, i) - 2)
                sp.dma_start(ring[:, 4 + s, :].rearrange("p (t n) -> p t n", t=2), src).then_inc(full[4 + s], 16)

            def gate_up(e, c):
                return gu_v[bass.ds(e, 1), c, :, :].rearrange("o p (t n) -> (o p) t n", t=2)

            def load_down(e, place, i):
                for k in range(4):
                    load_chunk(dn_v[bass.ds(e, 1), k, :, :, :].rearrange("o p t n -> (o p) t n"), place + k, i)

            sp.wait_ge(sem["att_done"], 1)
            sp.wait_ge(sem["own_turned"], NS)
            for t, (r0, n) in enumerate(TILES):
                sp.dma_start(h_nat[0:n, t, :], x_rows[t]).then_inc(sem["xres_loaded"], 16)
            sp.dma_start(router_w, w_router.rearrange("o (k p) e -> p (o k) e", p=P))\
                .then_inc(sem["late_loaded"], 16)
            sp.dma_start(br_row, row(b_router)).then_inc(sem["late_loaded"], 16)
            sp.dma_start(bgu_nat, b_gate_up.rearrange("o (a e) (j p) -> (o e j) a p", p=P, a=4))\
                .then_inc(sem["late_loaded"], 16)
            sp.dma_start(bd_nat, b_down[0, :, :]).then_inc(sem["bdown_loaded"], 16)
            for line, par in ((ln_g, ln1_g), (ln_b, ln1_b)):
                sp.dma_start(line, row(par)).then_inc(sem["ln1_loaded"], 16)
            for c in range(SLOTS):
                load_chunk(gate_up(0, c), 4 + c, 0, first=True)
            for w in (1, 2):
                for c in range(4):
                    load_w(proj_w[w][:, :, 256 * c:256 * (c + 1)], SEC + w, c)
            for c in range(SLOTS, KT):
                load_chunk(gate_up(0, c), 4 + c, 0)
            with sp.Fori(1, E) as e:
                for c in range(KT):
                    load_chunk(gate_up(e, c), c, e)
                load_down(e - 1, KT, e)
            sp.wait_ge(sem["items_ready"], 1)
            n_extra = sp.value_load(items[0:1, LIST - 1, 0:1], min_val=0, max_val=N_EXTRA)
            n_items = n_extra + E

            def expert_of(i):
                return sp.value_load(items[0:1, bass.ds(i, 1), 0:1].rearrange("o a b -> o (a b)"),
                                     min_val=0, max_val=E - 1)

            with sp.If(n_extra):
                with sp.Fori(E, n_items) as i:
                    e = expert_of(i)
                    for c in range(KT):
                        load_chunk(gate_up(e, c), c, i)
                    load_down(expert_of(i - 1), KT, i)
            load_down(expert_of(n_items - 1), 0, n_items)
            for t, (r0, n) in enumerate(TILES):
                sp.wait_ge(sem["y_done"], t + 1)
                sp.dma_start(y_rows[t], y_nat[0:n, t, :]).then_inc(sem["y_stored"], 16)
            sp.wait_ge(sem["y_stored"], 16 * NT)
            sp.wait_ge(sem["conv_stored"], 16 * 3)

        @block.gpsimd
        def _(pool):
            def fence():
                pool.drain()

            nc.gpsimd.memset(ident[:, :], 1.0)
            nc.gpsimd.memset(tri[:, :], 1.0)
            nc.gpsimd.memset(ones_after[:, :], 1.0)
            nc.gpsimd.memset(cmask[:, :], 0.0)
            nc.gpsimd.memset(smask[:, :, :], 0.0)
            nc.gpsimd.memset(blk[:, :], 1.0)
            nc.gpsimd.memset(small[:, :], 0.0)
            nc.gpsimd.memset(S_smp[:, NPG, :], NEG)
            fence()
            nc.gpsimd.affine_select(out=ident[:, :], in_=ident[:, :], pattern=[[-1, P]], base=0,
                                    channel_multiplier=1, compare_op=ALU.is_equal, fill=0.0)
            nc.gpsimd.affine_select(out=tri[:, :], in_=tri[:, :], pattern=[[1, P]], base=0,
                                    channel_multiplier=-1, compare_op=ALU.is_ge, fill=0.0)
            nc.gpsimd.affine_select(out=after, in_=after, pattern=[[-1, P]], base=0,
                                    channel_multiplier=1, compare_op=ALU.is_gt, fill=0.0)
            for a in (0, 2):
                m = cmask[:, a * P:(a + 1) * P]
                nc.gpsimd.affine_select(out=m, in_=m, pattern=[[-1, P]], base=0,
                                        channel_multiplier=1, compare_op=ALU.is_ge, fill=NEG)
            nc.gpsimd.affine_select(out=smask[:, :, :], in_=smask[:, :, :], pattern=[[-1, NS], [0, H]], base=0,
                                    channel_multiplier=1, compare_op=ALU.is_equal, fill=NEG)
            nc.gpsimd.affine_select(out=blk[:, :], in_=blk[:, :], pattern=[[1 - W, 4]], base=0,
                                    channel_multiplier=1, compare_op=ALU.is_ge, fill=0.0)
            fence()
            nc.gpsimd.affine_select(out=blk[:, :], in_=blk[:, :], pattern=[[W - 1, 4]], base=W - 2,
                                    channel_multiplier=-1, compare_op=ALU.is_ge, fill=0.0)
            nc.gpsimd.iota(items[:, :, :], pattern=[[1, LIST], [0, 2]], base=0, channel_multiplier=0)
            fence()
            nc.gpsimd.memset(items[:, :, 1:2].bitcast(F32), 0.0)
            nc.gpsimd.iota(kidx, pattern=[[0, 1]], base=0, channel_multiplier=1,
                           allow_small_or_imprecise_dtypes=True)
            pool.drain().then_inc(sem["pool_consts"], 1)

            def key_products(s, par, n_par):
                pool.wait_ge(qb_full[par], n_par * 16 + 16)
                for j, g in enumerate(POOL_PAGES):
                    pool.wait_ge(full[4 + g // 2], s * 32 + 32)
                    pool.wait_ge(sem["prodP_free"], s * len(POOL_PAGES) + (j + 1))
                    nc.gpsimd.tensor_tensor(prodP[j % 2], ring[:, 4 + g // 2, (g % 2) * D:(g % 2 + 1) * D],
                                            qb[par], ALU.mult).then_inc(sem["prodP_full"], 1)

            with pool.Fori(0, NS // 2) as i:
                for par in range(2):
                    key_products(i * 2 + par, par, i)

            pool.wait_ge(sem["kv_copied"], 4 * NT)
            pool.wait_ge(sem["logf_done"], 1)
            pool.wait_ge(sem["q_stored"], 16)
            pool.wait_ge(sem["self_done"], 1)
            pool.wait_ge(sem["bias_mm"], 1)
            pool.wait_ge(sem["sum_part"], 1)

            def stage(i, par):
                pool.wait_ge(sem["prompt_read"], i + 1)
                nc.gpsimd.tensor_copy(q_st[par], proj[:, bass.ds(i * TOK, SEQ)])
                nc.gpsimd.tensor_copy(k_st[par], proj[:, bass.ds(i * TOK + CH, SEQ)])
                nc.gpsimd.tensor_copy(v_st[par], v_nat[:, 0:2, bass.ds(i * P, P)])
                nc.gpsimd.tensor_copy(p_st[par], S_smp[:, :, bass.ds(i * H, H)])
                for hh in range(2):
                    f = [logf[:, t, bass.ds(i * 2 + hh, 1)].to_broadcast([P, P]) for t in range(2)]
                    nc.gpsimd.tensor_tensor(decay[par][:, hh, 0, :], tri[:, :], f[0], ALU.mult)
                    nc.gpsimd.tensor_tensor(decay[par][:, hh, 1, :], onesm, f[0], ALU.mult)
                    nc.gpsimd.tensor_tensor(decay[par][:, hh, 2, :], tri[:, :], f[1], ALU.mult)
                pool.drain().then_inc(sem["staged"], 1)

            with pool.Fori(0, H // 4) as i:
                stage(i * 2, 0)
                stage(i * 2 + 1, 1)
            pool.wait_ge(sem["att_done"], 1)
            pool.wait_ge(sem["v_mm"], NS)
            nc.gpsimd.iota(iota_f, pattern=[[1, 6 * CAP]], base=0, channel_multiplier=0,
                           allow_small_or_imprecise_dtypes=True)
            nc.gpsimd.memset(rt[:, :], 0.0)
            nc.gpsimd.tensor_tensor(tri_s, tri[:, :], ident[:, :], ALU.subtract)
            nc.gpsimd.tensor_tensor(sum_halves, ident[:, 0:CAP], ident[:, CAP:2 * CAP], ALU.add)
            pool.drain().then_inc(sem["pool_consts"], 1)
            for t, (r0, n) in enumerate(TILES):
                pool.wait_ge(sem["h_hi_done"], t + 1)
                nc.gpsimd.tensor_tensor(h_lo[0:n, t, :], h_nat[0:n, t, :], h_hi[0:n, t, :], ALU.subtract)\
                    .then_inc(sem["h_lo_done"], 1)
            pool.wait_ge(sem["items_ready"], 1)
            n_items = pool.value_load(items[0:1, LIST - 1, 0:1], min_val=0, max_val=N_EXTRA) + E

            def split_low(place, i):
                p = pair_of(place)
                pool.wait_ge(hi_done[p], split(place, i))
                nc.gpsimd.tensor_tensor(w_lo[p][:, :], ring[:, 4 + slot_of(place), :], w_hi[p][:, :],
                                        ALU.subtract).then_inc(lo_done[p], 1)

            for place in POOL_SPLITS[1:]:
                split_low(place, 0)
            with pool.Fori(1, n_items) as i:
                for place in POOL_SPLITS:
                    split_low(place, i)

        @block.tensor
        def _(pe):
            mm, tr = nc.tensor.matmul, nc.tensor.transpose

            pe.wait_ge(sem["pool_consts"], 1)
            pe.wait_ge(sem["x_loaded"], 16 * NT)
            for t, (r0, n) in enumerate(TILES):
                for half in range(2):
                    b = 2 * t + half
                    if b >= 2:
                        pe.wait_ge(sem["x_copied"], b - 1)
                    for k in range(4):
                        c0 = (4 * half + k) * P
                        last = tr(bank(2 + b % 2, 4)[:, k, 0:n], x_nat[0:n, t, c0:c0 + P], ident[0:n, 0:n])
                    last.then_inc(sem["x_turned"], 1)
            pe.wait_ge(sem["params_loaded"], 16 * 10)
            for k in range(KT):
                tr(pb[5][:, k * W:(k + 1) * W], convw_nat[:, k * P:(k + 1) * P], ident[0:W, 0:W])
            tr(pb[5][:, 256:256 + 3 * KT], cpar_nat, ident[0:3 * KT, 0:3 * KT])\
                .then_inc(sem["params_turned"], 1)
            pe.wait_ge(sem["smp_products"], 1)
            for k in range(KT):
                for i in range(2):
                    c0 = k * NS + 4 * i
                    last = mm(pb[7][:, c0:c0 + 4], state_nat[:, i, k * P:(k + 1) * P], blk[0:SR, :],
                              start=True, stop=True)
            last.then_inc(sem["smp_conv_mm"], 1)
            pe.wait_ge(sem["forget_loaded"], 32)
            pe.wait_ge(sem["x_copied"], 2 * NT)
            for t, (r0, n) in enumerate(TILES):
                for k in range(KT):
                    last = mm(pb[6][0:n, t * H:(t + 1) * H], xT[:, k, r0:r0 + n], wf[:, k, :],
                              start=(k == 0), stop=(k == KT - 1))
            last.then_inc(sem["logit_mm"], 1)

            def project(s, src, slots_done, used, tiles0):
                for m in range(8):
                    c = m // 2
                    if m % 2 == 0:
                        pe.wait_ge(full[c], slots_done * 16 + 16)
                    pe.wait_ge(used, tiles0 + (m + 1))
                    w = ring[:, c, :].rearrange("p (k n) -> p k n", k=KT)
                    for k in range(KT):
                        last = mm(pb[m % 2][:, 0:TOK], w[:, k, (m % 2) * P:(m % 2 + 1) * P], src[:, k, :],
                                  start=(k == 0), stop=(k == KT - 1))
                    last.then_inc(sem["proj_done"] if m % 2 == 0 else free[c], 1)

            def section(s):
                project(s, xT, s, sem["proj_used"], s * 8)

            section(0)
            pe.wait_ge(sem["proj_used"], 2 + 8)
            for k in range(KT):
                last = tr(bank(2 + k // 4, 4)[0:NS, k % 4, :], qT[:, k, SEQ:TOK], ident[:, :])
            last.then_inc(sem["q_turned"], 1)
            with pe.Fori(1, 3) as s:
                section(s)
            pe.wait_ge(sem["proj_used"], 2 + 24)
            pe.wait_ge(sem["q_copied"], 2)
            for i, src in enumerate((kT, vT)):
                for t, (r0, n) in enumerate(TILES):
                    for half in range(2):
                        b = 6 * i + 2 * t + half
                        if b >= 2:
                            pe.wait_ge(sem["kv_copied"], b - 1)
                        for k in range(4):
                            last = tr(bank(2 + b % 2, 4)[0:n, k, :], src[:, 4 * half + k, r0:r0 + n], ident[:, :])
                        last.then_inc(sem["kv_turned"], 1)
            with pe.Fori(3, SEC) as s:
                section(s)
            pe.wait_ge(sem["after_sums"], 1)
            for half in range(2):
                a, b = 4 * half, 4 * half + 4
                mm(pb[4 + half][:, :], after, lf[:, a:b, :], start=True, stop=False)
                last = mm(pb[4 + half][:, :], onesm, lf_after[:, a:b, :], start=False, stop=True)
            last.then_inc(sem["bias_mm"], 1)
            pe.wait_ge(sem["max_part"], 1)
            pe.wait_ge(sem["kv_copied"], 4 * NT)
            tr(pb[2][:, 0:SH], part, ident[:, :]).then_inc(sem["max_turned"], 1)
            pe.wait_ge(sem["max_diag"], 1)
            mm(pb[3][:, 0:SH], onesm, part, start=True, stop=True).then_inc(sem["max_spread"], 1)
            pe.wait_ge(sem["sum_part"], 1)
            mm(pb[2][:, 0:SH], onesm, part, start=True, stop=True).then_inc(sem["sum_spread"], 1)
            pe.wait_ge(sem["sample_exps"], 1)

            def values(s, par, n_par, pages):
                for g in pages:
                    if g < NPG:
                        buf = 4 + 4 * par + g // 2
                        if g % 2 == 0:
                            pe.wait_ge(full[buf], n_par * 32 + (32 * K_USES + 32 if par == 0 else 32))
                        v = ring[:, buf, (g % 2) * D:(g % 2 + 1) * D]
                    else:
                        v = v_nat[0:NS, 2, :]
                    rows = v.shape[0]
                    for half in range(2):
                        last = mm(pb[5 + half][0:H, :], p_st[par][0:rows, g, :], v[:, half * 512:(half + 1) * 512],
                                  start=(g == 0), stop=(g == NPG))
                    if g < NPG and g % 2 == 1:
                        last.then_inc(free[buf], 1)
                    elif g == NPG:
                        last.then_inc(sem["v_mm"], 1)

            def head_pair(i, s, par):
                pe.wait_ge(sem["staged"], i + 1)
                for hh in range(2):
                    pe.wait_ge(sem["probs_done"], i * 2 + (hh + 1))
                    r = slice(64 * hh, 64 * hh + 64)
                    s0, s1 = pb[hh][:, 0:P], pb[hh][:, P:3 * P]
                    mm(s0, q_st[par][r, 0:P], k_st[par][r, 0:P], start=True, stop=False)
                    mm(s0, decay[par][:, hh, 0, :], after, start=False, stop=True)
                    mm(s1, q_st[par][r, P:2 * P], k_st[par][r, :], start=True, stop=False)
                    mm(s1[:, 0:P], decay[par][:, hh, 1, :], after, start=False, stop=False)
                    mm(s1, decay[par][:, hh, 2, :], ones_after[:, :], start=False, stop=True).then_inc(sem["scores_mm"], 1)
                values(s, par, i_half, range(0, 6))
                for hh in range(2):
                    pe.wait_ge(sem["probs_done"], i * 2 + (hh + 3))
                    for j in range(3):
                        last = tr(bank(2 + hh, 4)[:, j, :], probs[:, hh, j * P:(j + 1) * P], ident[:, :])
                    last.then_inc(sem["turned_mm"], 1)
                values(s, par, i_half, range(6, NPG + 1))
                pe.wait_ge(sem["oT_copied"], i + 1)
                for hh in range(2):
                    pe.wait_ge(sem["probsT_copied"], i * 2 + (hh + 1))
                    o = pb[4][64 * hh:64 * hh + 64, 0:SEQ]
                    v = v_st[par][:, :, 64 * hh:64 * hh + 64]
                    mm(o, v[:, 0, :], probsT[:, hh, 0:2 * P], start=True, stop=False)
                    last = mm(o[:, P:2 * P], v[:, 1, :], probsT[:, hh, 2 * P:3 * P], start=False, stop=True)
                last.then_inc(sem["prompt_read"], 1)
                pe.wait_ge(sem["own_masked"], s + 1)
                pe.wait_ge(sem["smp_out"], s + 1)
                for hp in range(H // 2):
                    last = mm(pb[7][:, hp:hp + 1], own_heads[:, hp * P:(hp + 1) * P], onesm[0:H, 0:1],
                              start=True, stop=True)
                last.then_inc(sem["own_turned"], 1)

            with pe.Fori(0, NS // 2) as i_half:
                for par in range(2):
                    head_pair(i_half * 2 + par, i_half * 2 + par, par)
            pe.wait_ge(sem["conv_done"], KT // 2)
            for k in range(KT):
                last = mm(pb[6][:, 0:TOK], onesm, y_conv[:, k, :], start=(k == 0), stop=(k == KT - 1))
            last.then_inc(sem["mean_mm"], 1)
            for j, (a, b) in enumerate(((SEQ - (W - 1), SEQ), (SEQ, TOK))):
                if j == 1:
                    pe.wait_ge(sem["uout_copied"], 2)
                for k in range(KT):
                    last = tr(bank(2 + k // 4, 4)[0:b - a, k % 4, :], u_val[:, k, a:b], ident[:, :])
                last.then_inc(sem["uout_turned"], 1)
            pe.wait_ge(sem["att_done"], 1)
            pe.wait_ge(sem["smp_out"], NS + 1)
            project(0, attT, SEC, sem["gated"], 0)
            pe.wait_ge(sem["squares"], 1)
            for k in range(KT):
                last = mm(pb[7][:, 0:TOK], onesm, squares[:, k, :], start=(k == 0), stop=(k == KT - 1))
            last.then_inc(sem["var_mm"], 1)
            pe.wait_ge(sem["late_loaded"], 48)
            for a in range(4):
                last = tr(bank(4, 4)[:, a, :], bgu_nat[:, a, :], ident[:, :])
            last.then_inc(sem["b_turned"], 1)
            pe.wait_ge(sem["conv_act"], 1)
            project(0, y_conv, SEC + 1, sem["gated"], 8)
            pe.wait_ge(sem["gated"], 2 + 16)
            project(0, mT, SEC + 2, sem["mixT_copied"], 0)
            for t, (r0, n) in enumerate(TILES):
                for half in range(2):
                    b = 2 * t + half
                    pe.wait_ge(sem["mixT_copied"], 2 + 8)
                    if b >= 2:
                        pe.wait_ge(sem["resid"], b - 1)
                    else:
                        pe.wait_ge(sem["uout_copied"], 4)
                    for k in range(4):
                        last = tr(bank(2 + b % 2, 4)[0:n, k, :], mixT[:, 4 * half + k, r0:r0 + n], ident[:, :])
                    last.then_inc(sem["mix_turned"], 1)
            for t, (r0, n) in enumerate(TILES):
                pe.wait_ge(sem["h_done"], t + 1)
                pe.wait_ge(sem["b_copied"], 1)
                for half in range(2):
                    b = 2 * t + half
                    if b >= 2:
                        pe.wait_ge(sem["hT_copied"], b - 1)
                    for k in range(4):
                        c0 = (4 * half + k) * P
                        last = tr(bank(4 + b % 2, 4)[:, k, 0:n], h_nat[0:n, t, c0:c0 + P], ident[0:n, 0:n])
                    last.then_inc(sem["h_turned"], 1)
            pe.wait_ge(sem["hT_copied"], 2 * NT)
            for t, (r0, n) in enumerate(TILES):
                for k in range(KT):
                    last = mm(pb[6][0:n, t * E:(t + 1) * E], hT[:, k, r0:r0 + n], router_w[:, k, :],
                              start=(k == 0), stop=(k == KT - 1))
            last.then_inc(sem["router_mm"], 1)
            pe.wait_ge(sem["mask_done"], 1)
            pe.wait_ge(sem["pool_consts"], 2)
            for t, (r0, n) in enumerate(TILES):
                for j in range(t + 1):
                    rows = TILES[j][1]
                    lhs = tri_s if j == t else onesm
                    last = mm(pb[7][0:n, t * E:(t + 1) * E], lhs[0:rows, 0:n], mask[0:rows, j, :],
                              start=(j == 0), stop=(j == t))
            for j, (_, rows) in enumerate(TILES):
                last = mm(pb[7][:, 3 * E:4 * E], onesm[0:rows, :], mask[0:rows, j, :],
                          start=(j == 0), stop=(j == NT - 1))
            last.then_inc(sem["rank_mm"], 1)
            pe.wait_ge(sem["weights_done"], 1)
            for t, (r0, n) in enumerate(TILES):
                last = tr(pb[2][0:E, r0:r0 + n], wts[0:n, t, :], ident[0:n, 0:n])
            last.then_inc(sem["wT_turned"], 1)
            pe.wait_ge(sem["wT_copied"], 1)
            pe.wait_ge(sem["bdown_loaded"], 16)
            for k in range(KT):
                if k >= 2:
                    pe.wait_ge(sem["acc_init"], k - 1)
                mm(pb[k % 2][:, 0:TOK], bd_nat[:, k * P:(k + 1) * P], wcT, start=True, stop=True)\
                    .then_inc(sem["bdown_mm"], 1)

            def gather(n):
                pe.wait_ge(sem["sel_ready"], n + 1)
                for half in range(2):
                    for h_part, c0 in ((h_hi, CAP), (h_lo, 0)):
                        for t, (r0, rows) in enumerate(TILES):
                            last = mm(pb[6 + half][:, :], sel[0:rows, t, c0:c0 + 2 * CAP],
                                      h_part[0:rows, t, half * 512:(half + 1) * 512],
                                      start=h_part is h_hi and t == 0, stop=h_part is h_lo and t == NT - 1)
                last.then_inc(sem["gather_mm"], 1)

            def turn_tokens(n):
                pe.wait_ge(sem["rows_copied"], n * 2 + 2)
                for k in range(KT):
                    last = mm(bank(6 + k // 4, 4)[:, k % 4, :], x_rows_r[:, k * P:(k + 1) * P], ident_r[:, :],
                              start=True, stop=True)
                last.then_inc(sem["tokens_turned"], 1)

            def scatter(n, tiles):
                for k in tiles:
                    pe.wait_ge(sem["scatter_added"], n * KT + (k + 1))
                    mm(pb[4 + k % 2][:, 0:TOK], out_sb[:, k * P:(k + 1) * P], selT, start=True, stop=True)\
                        .then_inc(sem["scatter_mm"], 1)

            def turn_columns(n):
                pe.wait_ge(sem["selw_ready"], n + 1)
                for t, (r0, rows) in enumerate(TILES):
                    last = tr(pb[6][:, r0:r0 + rows], selw[0:rows, t, :], ident[0:rows, 0:rows])
                last.then_inc(sem["selw_turned"], 1)

            pe.wait_ge(sem["h_lo_done"], NT)
            gather(0)
            turn_tokens(0)
            pe.wait_ge(sem["acc_init"], KT)
            pe.wait_ge(sem["items_ready"], 1)
            n_items = pe.value_load(items[0:1, LIST - 1, 0:1], min_val=0, max_val=N_EXTRA) + E

            def gate_up(i, c, place):
                p = pair_of(place)
                for w, done in ((w_hi[p], hi_done[p]), (w_lo[p], lo_done[p])):
                    pe.wait_ge(done, split(place, i))
                    for b in range(4):
                        last = mm(pb[b][:, :], xg[:, c, :], w[:, b * 512:(b + 1) * 512],
                                  start=c == 0 and w is w_hi[p], stop=c == KT - 1 and w is w_lo[p])
                last.then_inc(pair_free[p], 1)

            def turn_gate_up(half):
                for j in range(KT):
                    last = mm(bank(4 + half, KT)[:, j, :], gu_sb[:, (half * KT + j) * P:(half * KT + j + 1) * P],
                              sum_halves, start=True, stop=True)
                last.then_inc(sem["gu_turned"], 1)

            def down(i, place):
                pe.wait_ge(sem["act_ready"], i)
                for k in range(4):
                    p = pair_of(place + k)
                    for w, done in ((w_hi[p], hi_done[p]), (w_lo[p], lo_done[p])):
                        pe.wait_ge(done, split(place + k, i))
                        for j in range(4):
                            last = mm(pb[4 + j % 2][:, :], act2[:, 2 * k + j // 2, :], w[:, j * 512:(j + 1) * 512],
                                      start=k == 0 and w is w_hi[p] and j < 2,
                                      stop=k == 3 and w is w_lo[p] and j >= 2)
                    last.then_inc(pair_free[p], 1)

            pe.wait_ge(sem["xg_ready"], 2)
            for c in range(KT):
                gate_up(0, c, 4 + c)
            gather(1)
            turn_tokens(1)
            with pe.Fori(1, n_items) as i:
                pe.wait_ge(sem["xg_ready"], i * 2 + 2)
                turn_columns(i - 1)
                pe.wait_ge(sem["gu_copied"], i * 4)
                gate_up(i, 0, 0)
                pe.wait_ge(sem["out_copied"], i * 2)
                turn_gate_up(0)
                gate_up(i, 1, 1)
                turn_gate_up(1)
                gate_up(i, 2, 2)
                gate_up(i, 3, 3)
                pe.wait_ge(sem["selT_copied"], i)
                gather(i + 1)
                gate_up(i, 4, 4)
                gate_up(i, 5, 5)
                turn_tokens(i + 1)
                pe.wait_ge(sem["gate_ready"], i)
                scatter(i - 1, range(0, 3))
                gate_up(i, 6, 6)
                scatter(i - 1, range(3, 6))
                gate_up(i, 7, 7)
                scatter(i - 1, range(6, 8))
                pe.wait_ge(sem["scatter_added"], i * KT + 2)
                down(i, KT)
            pe.wait_ge(sem["gu_copied"], n_items * 4)
            pe.wait_ge(sem["out_copied"], n_items * 2)
            turn_gate_up(0)
            turn_gate_up(1)
            pe.wait_ge(sem["xg_ready"], n_items * 2 + 2)
            turn_columns(n_items - 1)
            pe.wait_ge(sem["gate_ready"], n_items)
            pe.wait_ge(sem["selT_copied"], n_items)
            scatter(n_items - 1, range(KT))
            pe.wait_ge(sem["scatter_added"], n_items * KT + 2)
            down(n_items, 0)
            pe.wait_ge(sem["out_copied"], n_items * 2 + 2)
            turn_columns(n_items)
            pe.wait_ge(sem["selT_copied"], n_items + 1)
            scatter(n_items, range(KT))
            for t, (r0, n) in enumerate(TILES):
                pe.wait_ge(sem["scatter_added"], n_items * KT + (KT + 2))
                for half in range(2):
                    b = 2 * t + half
                    if b >= 2:
                        pe.wait_ge(sem["resid"], 2 * NT + b - 1)
                    for k in range(4):
                        last = tr(bank(b % 2, 4)[0:n, k, :], accT[:, 4 * half + k, r0:r0 + n], ident[:, :])
                    last.then_inc(sem["y_turned"], 1)

        @block.scalar
        def _(act):
            def copy(out, in_, scale=None):
                if scale is None:
                    return nc.scalar.copy(out, in_)
                return nc.scalar.activation(out, in_, ACT.Copy, scale=scale)

            act.sem_inc(sem["proj_used"], 2)
            act.sem_inc(sem["mixT_copied"], 2)
            act.sem_inc(sem["oT_copied"], 1)
            for t, (r0, n) in enumerate(TILES):
                for half in range(2):
                    b = 2 * t + half
                    act.wait_ge(sem["x_turned"], b + 1)
                    copy(xT[:, 4 * half:4 * half + 4, r0:r0 + n], bank(2 + b % 2, 4)[:, :, 0:n])\
                        .then_inc(sem["x_copied"], 1)
            act.wait_ge(sem["params_turned"], 1)
            copy(cw[:, :, :], pb[5][:, 0:KT * W].rearrange("p (k w) -> p k w", w=W))
            copy(cpar[:, :], pb[5][:, 256:256 + 3 * KT]).then_inc(sem["params_copied"], 1)
            act.wait_ge(sem["smp_conv_mm"], 1)
            act.wait_ge(sem["pool_consts"], 1)
            copy(smp_conv, pb[7][:, 0:KT * NS].rearrange("p (c b) -> p c b", b=NS))
            act.wait_ge(sem["neg_abs"], 1)
            nc.scalar.activation(na, na, ACT.Exp)
            act.drain()
            nc.scalar.activation(na, na, ACT.Ln, bias=1.0).then_inc(sem["softplus"], 1)

            def store_section(s, scale=None):
                for m in range(8):
                    if m % 2 == 0:
                        act.wait_ge(sem["proj_done"], s * 4 + (m // 2 + 1))
                    else:
                        act.wait_ge(free[m // 2], s + 2)
                    copy(proj[:, bass.ds(s * CH + m * TOK, TOK)], pb[m % 2][:, 0:TOK], scale)\
                        .then_inc(sem["proj_used"], 1)

            store_section(0, SCALE)
            act.wait_ge(sem["logf_done"], 1)
            act.dma_start(lfp_rows, logf[:, 0:2, :]).then_inc(sem["logf_stored"], 16)
            act.dma_start(lfs_rows, logf[0:NS, 2, :]).then_inc(sem["logf_stored"], 16)
            act.wait_ge(sem["q_turned"], 1)
            for half in range(2):
                copy(q_nat[:, 512 * half:512 * (half + 1)], pb[2 + half][0:NS, :]).then_inc(sem["q_copied"], 1)
            act.wait_ge(sem["q_copied"], 2)
            act.dma_start(q_scratch, q_nat).then_inc(sem["q_stored"], 16)
            with act.Fori(1, 3) as s:
                store_section(s)
            for i, (dst, rows) in enumerate(((k_nat, k_rows), (v_nat, v_rows))):
                for t, (r0, n) in enumerate(TILES):
                    for half in range(2):
                        b = 6 * i + 2 * t + half
                        act.wait_ge(sem["kv_turned"], b + 1)
                        copy(dst[0:n, t, 512 * half:512 * (half + 1)], pb[2 + b % 2][0:n, :])\
                            .then_inc(sem["kv_copied"], 1)
                    act.wait_ge(sem["kv_copied"], 6 * i + 2 * t + 2)
                    act.dma_start(rows[t], dst[0:n, t, :]).then_inc(sem["kv_stored"], 16)
            with act.Fori(3, 5) as s:
                store_section(s)
            act.wait_ge(sem["proj_used"], 2 + 40)
            nc.scalar.activation(u_gate, u_gate, ACT.Sigmoid).then_inc(sem["u_sig"], 1)
            with act.Fori(5, SEC) as s:
                store_section(s)
            act.wait_ge(sem["proj_used"], 2 + 56)
            for g in (g_att, g_conv):
                last = nc.scalar.activation(g, g, ACT.Sigmoid)
            last.then_inc(sem["gates"], 1)
            act.wait_ge(sem["shifted"], 1)
            nc.scalar.activation(S_smp[:, :, :], S_smp[:, :, :], ACT.Exp).then_inc(sem["sample_exps"], 1)

            def softmax_pair(i):
                for hh in range(2):
                    act.wait_ge(sem["row_max"], i * 2 + (hh + 1))
                    for j, (a, b) in enumerate(((0, P), (P, 3 * P))):
                        last = nc.scalar.activation(probs[:, hh, a:b], probs[:, hh, a:b], ACT.Exp,
                                                    bias=nmax[:, hh, j:j + 1], accum_out=psums[:, hh, j:j + 1])
                    last.then_inc(sem["exps"], 1)
                for hh in range(2):
                    act.wait_ge(sem["turned_mm"], i * 2 + (hh + 1))
                    copy(probsT[:, hh, :], pb[2 + hh][:, 0:3 * P]).then_inc(sem["probsT_copied"], 1)
                act.wait_ge(sem["prompt_read"], i + 3)
                copy(attT[:, bass.ds(i, 1), 0:SEQ].rearrange("p a t -> p (a t)"), pb[4][:, 0:SEQ])\
                    .then_inc(sem["oT_copied"], 1)

            with act.Fori(0, H // 2) as i:
                softmax_pair(i)
            act.drain().then_inc(sem["att_done"], 1)
            for j, dst in enumerate((uout_p, uout_s)):
                act.wait_ge(sem["uout_turned"], j + 1)
                for half in range(2):
                    copy(dst[:, 512 * half:512 * (half + 1)], pb[2 + half][0:dst.shape[0], :])\
                        .then_inc(sem["uout_copied"], 1)
                act.wait_ge(sem["uout_copied"], 2 * j + 2)
                act.dma_start(conv_prompt[0, 0, :, :] if j == 0 else conv_sample[0, :, W - 2, :], dst)\
                    .then_inc(sem["conv_stored"], 16)
            act.wait_ge(sem["centred"], 1)
            nc.scalar.activation(squares, y_conv, ACT.Square).then_inc(sem["squares"], 1)
            act.wait_ge(sem["var_done"], 1)
            nc.scalar.activation(pb[7][:, 0:TOK], pb[7][:, 0:TOK], ACT.Sqrt).then_inc(sem["std_done"], 1)
            act.wait_ge(sem["b_turned"], 1)
            copy(bias_gu, pb[4][:, :]).then_inc(sem["b_copied"], 1)
            act.wait_ge(sem["normed"], 1)
            for k in range(KT):
                last = nc.scalar.activation(y_conv[:, k, :], y_conv[:, k, :], ACT.Silu,
                                            bias=cpar[:, 2 * KT + k:2 * KT + k + 1],
                                            scale=cpar[:, KT + k:KT + k + 1])
            last.then_inc(sem["conv_act"], 1)
            for m in range(8):
                if m % 2 == 0:
                    act.wait_ge(sem["proj_done"], 4 * (SEC + 2) + (m // 2 + 1))
                else:
                    act.wait_ge(free[m // 2], SEC + 4)
                copy(mixT[:, m, :], pb[m % 2][:, 0:TOK]).then_inc(sem["mixT_copied"], 1)

            def std(turn):
                act.wait_ge(sem["row_var"], turn + 1)
                nc.scalar.activation(rstd, rstd, ACT.Sqrt).then_inc(sem["row_std"], 1)

            def hT_copy(t):
                n, r0 = TILES[t][1], TILES[t][0]
                for half in range(2):
                    b = 2 * t + half
                    act.wait_ge(sem["h_turned"], b + 1)
                    copy(hT[:, 4 * half:4 * half + 4, r0:r0 + n], bank(4 + b % 2, 4)[:, :, 0:n])\
                        .then_inc(sem["hT_copied"], 1)

            def h_high(t):
                n = TILES[t][1]
                act.wait_ge(sem["h_done"], t + 1)
                copy(h_hi[0:n, t, :], h_nat[0:n, t, :]).then_inc(sem["h_hi_done"], 1)

            act.wait_ge(sem["kv_stored"], 16 * 2 * NT)
            act.wait_ge(sem["v_mm"], NS)
            for t in range(NT):
                std(t)
                if t:
                    hT_copy(t - 1)
                    h_high(t - 1)
            hT_copy(NT - 1)
            h_high(NT - 1)
            act.wait_ge(sem["logits_max"], 1)
            for t in range(NT):
                last = nc.scalar.activation(wts[:, t, :], logits[:, t, :], ACT.Exp, bias=nbig[:, t:t + 1])
            last.then_inc(sem["exps_r"], 1)
            act.wait_ge(sem["wT_turned"], 1)
            copy(wcT, pb[2][0:E, 0:TOK]).then_inc(sem["wT_copied"], 1)

            def copy_rows(n):
                act.wait_ge(sem["gather_mm"], n + 1)
                for half in range(2):
                    copy(x_rows_r[:, 512 * half:512 * (half + 1)], pb[6 + half][:, :])\
                        .then_inc(sem["rows_copied"], 1)

            def gathered(n):
                act.wait_ge(sem["tokens_turned"], n + 1)
                for half in range(2):
                    copy(xg[:, 4 * half:4 * half + 4, :], bank(6 + half, 4)).then_inc(sem["xg_ready"], 1)

            def split_high(place, i):
                p, s = pair_of(place), slot_of(place)
                act.wait_ge(full[4 + s], loaded(place, i))
                act.wait_ge(pair_free[p], used(place, i) - 1)
                copy(w_hi[p][:, :], ring[:, 4 + s, :]).then_inc(hi_done[p], 1)

            def copy_out(i, last_place):
                act.wait_ge(pair_free[pair_of(last_place)], used(last_place, i))
                for n in range(2):
                    copy(out_sb[:, n * 512:(n + 1) * 512], pb[4 + n][:, :]).then_inc(sem["out_copied"], 1)

            def copy_gate_up(i, last_place):
                act.wait_ge(pair_free[pair_of(last_place)], used(last_place, i))
                for b in (2, 3):
                    copy(gu_sb[:, b * 512:(b + 1) * 512], pb[b][:, :]).then_inc(sem["gu_copied"], 1)

            def sigmoid(i):
                act.wait_ge(sem["gate_ready"], i)
                nc.scalar.activation(s_buf, g_buf, ACT.Sigmoid, scale=SWIGLU_ALPHA).then_inc(sem["sigmoid_done"], 1)

            def copy_columns(n):
                act.wait_ge(sem["selw_turned"], n + 1)
                copy(selT, pb[6][:, 0:TOK]).then_inc(sem["selT_copied"], 1)

            act.wait_ge(sem["extras_made"], 1)
            act.dma_start(extras_scratch, extra_items[0:N_EXTRA + 2, :]).then_inc(sem["extras_stored"], 16)
            act.wait_ge(sem["extras_stored"], 16)
            act.dma_start(items[0:1, E:E + N_EXTRA + 2, :], extras_scratch.unsqueeze(0))\
                .then_inc(sem["extras_loaded"], 16)
            act.dma_start(items[0:1, LIST - 1, :], n_extra_i[:, :]).then_inc(sem["extras_loaded"], 16)
            act.wait_ge(sem["h_done"], NT)
            for line, par in ((ln_g, ln2_g), (ln_b, ln2_b)):
                act.dma_start(line, row(par)).then_inc(sem["ln2_loaded"], 16)
            act.wait_ge(sem["extras_loaded"], 32)
            act.sem_inc(sem["items_ready"], 1)
            copy_rows(0)
            gathered(0)
            for c in range(4):
                act.wait_ge(free[c], SEC + 4)
            n_items = act.value_load(items[0:1, LIST - 1, 0:1], min_val=0, max_val=N_EXTRA) + E
            for place in range(4, PLACES):
                split_high(place, 0)
            copy_gate_up(0, PLACES - 1)
            copy_rows(1)
            gathered(1)
            for place in (0, 1, 2):
                split_high(place, 1)
            with act.Fori(1, n_items) as i:
                copy_columns(i - 1)
                split_high(3, i)
                split_high(4, i)
                sigmoid(i)
                split_high(5, i)
                copy_rows(i + 1)
                for place in range(6, KT + 2):
                    split_high(place, i)
                copy_gate_up(i, KT - 1)
                gathered(i + 1)
                split_high(10, i)
                split_high(11, i)
                split_high(0, i + 1)
                split_high(1, i + 1)
                copy_out(i, PLACES - 1)
                split_high(2, i + 1)
            copy_columns(n_items - 1)
            sigmoid(n_items)
            split_high(3, n_items)
            copy_out(n_items, 3)
            copy_columns(n_items)
            for t in range(NT):
                std(NT + t)

        @block.vector
        def _(dve):
            v = nc.vector
            stt, tt, ts = v.scalar_tensor_tensor, v.tensor_tensor, v.tensor_scalar

            def fence():
                dve.drain()

            dve.sem_inc(sem["qb_free"], 1)
            dve.sem_inc(sem["qb_free"], 1)
            dve.sem_inc(sem["prodP_free"], 2)
            dve.sem_inc(sem["probs_done"], 2)
            dve.sem_inc(sem["gated"], 2)
            dve.sem_inc(sem["scatter_added"], 2)
            for p in range(3):
                dve.sem_inc(pair_free[p], 1)
            dve.sem_inc(sem["prompt_read"], 2)
            dve.sem_inc(sem["smp_out"], 1)
            dve.wait_ge(sem["params_loaded"], 16 * 10)
            for i in range(2):
                tt(state_nat[:, i, :], state_nat[:, i, :], cw_rows, ALU.mult)
            dve.drain().then_inc(sem["smp_products"], 1)
            dve.wait_ge(sem["pool_consts"], 1)
            dve.wait_ge(sem["logit_mm"], 1)
            dve.wait_ge(sem["forget_loaded"], 32)
            tt(zf[:, 0:2, :], pb[6][:, 0:2 * H].rearrange("p (t h) -> p t h", h=H),
               bf_row[:, :].unsqueeze(1).to_broadcast([P, 2, H]), ALU.add)
            tt(zf[0:NS, 2, :], pb[6][0:NS, 2 * H:3 * H], bf_row[0:NS, :], ALU.add)
            fence()
            stt(na, zf, -1.0, zf, ALU.mult, ALU.min).then_inc(sem["neg_abs"], 1)
            dve.wait_ge(sem["softplus"], 1)
            stt(logf, zf, 0.0, na, ALU.min, ALU.subtract).then_inc(sem["logf_done"], 1)

            def key_scores(s, par, n_par):
                dve.wait_ge(qb_full[par], n_par * 16 + 16)
                for r in range(4):
                    dve.wait_ge(full[4 + r], s * 32 + 32)
                    for g in (2 * r, 2 * r + 1):
                        if g not in POOL_PAGES:
                            tt(prodD[r % 2], ring[:, 4 + r, (g % 2) * D:(g % 2 + 1) * D], qb[par], ALU.mult)
                    for g in (2 * r, 2 * r + 1):
                        if g in POOL_PAGES:
                            j = POOL_PAGES.index(g)
                            dve.wait_ge(sem["prodP_full"], s * len(POOL_PAGES) + (j + 1))
                            v.tensor_reduce(S_smp[:, g, bass.ds(s * H, H)],
                                            prodP[j % 2].rearrange("p (h d) -> p h d", h=H), X, ALU.add)\
                                .then_inc(sem["prodP_free"], 1)
                    dve.drain().then_inc(free[4 + r], 1)
                    for g in (2 * r, 2 * r + 1):
                        if g not in POOL_PAGES:
                            v.tensor_reduce(S_smp[:, g, bass.ds(s * H, H)],
                                            prodD[r % 2].rearrange("p (h d) -> p h d", h=H), X, ALU.add)
                dve.drain().then_inc(sem["scores_done"], 1)
                dve.sem_inc(sem["qb_free"], 1)

            dve.wait_ge(sem["params_copied"], 1)
            with dve.Fori(0, NS // 2) as i:
                for par in range(2):
                    key_scores(i * 2 + par, par, i)
            dve.wait_ge(sem["kv_copied"], 2 * NT)
            tt(self_prod, q_nat, k_nat[0:NS, 2, :], ALU.mult)
            fence()
            v.tensor_reduce(self_s, self_prod.rearrange("p (h d) -> p h d", h=H), X, ALU.add)
            fence()
            tt(S_smp[0:NS, NPG, :].rearrange("p (s h) -> p s h", h=H), smask[:, :, :],
               self_s.unsqueeze(1).to_broadcast([NS, NS, H]), ALU.add).then_inc(sem["self_done"], 1)
            dve.wait_ge(sem["lf_loaded"], 16 * NS * NPG)
            v.memset(lf_after[:, NPG - 1, :], 0.0)
            for g in range(NPG - 2, -1, -1):
                fence()
                tt(lf_after[:, g, :], lf_after[:, g + 1, :], lf[:, g + 1, :], ALU.add)
            fence()
            dve.wait_ge(sem["logf_new_loaded"], 16)
            tt(lf_after[0:1, :, :], lf_after[0:1, :, :], logf_row[:, :].unsqueeze(1).to_broadcast([1, NPG, SH]),
               ALU.add).then_inc(sem["after_sums"], 1)
            dve.wait_ge(sem["bias_mm"], 1)
            for half in range(2):
                sl = S_smp[:, 4 * half:4 * half + 4, :]
                tt(sl, sl, bank(4 + half, 4), ALU.add)
            fence()
            v.tensor_reduce(part, S_smp[:, :, :].rearrange("p g n -> p n g"), X, ALU.max)\
                .then_inc(sem["max_part"], 1)
            dve.wait_ge(sem["max_turned"], 1)
            v.tensor_reduce(smax, pb[2][:, 0:SH], X, ALU.max)
            fence()
            ts(part, ident[:, :], smax, None, ALU.mult).then_inc(sem["max_diag"], 1)
            dve.wait_ge(sem["max_spread"], 1)
            tt(S_smp[:, :, :], S_smp[:, :, :], pb[3][:, 0:SH].unsqueeze(1).to_broadcast([P, NPG + 1, SH]),
               ALU.subtract).then_inc(sem["shifted"], 1)
            dve.wait_ge(sem["sample_exps"], 1)
            v.tensor_reduce(part, S_smp[:, :, :].rearrange("p g n -> p n g"), X, ALU.add)\
                .then_inc(sem["sum_part"], 1)
            dve.wait_ge(sem["sum_spread"], 1)
            v.reciprocal(part, pb[2][:, 0:SH])
            dve.wait_ge(sem["u_sig"], 1)
            tt(u_val, u_val, u_gate, ALU.mult)
            fence()
            dve.wait_ge(sem["logf_done"], 1)
            cwf = cw[:, :, :].rearrange("p k w -> p (k w)")
            smpf = small[:, 192:256]

            def conv_rounds(i, rounds):
                for d in rounds:
                    for a in range(2):
                        u0, w0 = (i * 2 + a) * TOK + 3 * CH, (i * 2 + a) * W + (W - 1)
                        late, w_d = late_sums[a], cwf[:, bass.ds(w0 - d, 1)]
                        if d == 0:
                            ts(proj[:, bass.ds(u0 + CH, TOK)], proj[:, bass.ds(u0, TOK)], w_d,
                               cpar[:, bass.ds(i * 2 + a, 1)], ALU.mult, ALU.add)
                        else:
                            acc = proj[:, bass.ds(u0 + (CH + d), SEQ - d)]
                            stt(acc, proj[:, bass.ds(u0, SEQ - d)], w_d, acc, ALU.mult, ALU.add)
                        if LATE + d < W:
                            w_l, n = cwf[:, bass.ds(w0 - LATE - d, 1)], SEQ - LATE - d
                            if d == 0:
                                ts(late, proj[:, bass.ds(u0, n)], w_l, None, ALU.mult)
                            else:
                                stt(late[:, d:], proj[:, bass.ds(u0, n)], w_l, late[:, d:], ALU.mult, ALU.add)
                    fence()

            def conv_end(i):
                for a in range(2):
                    y0 = (i * 2 + a) * TOK + 4 * CH
                    y_late, y_smp = proj[:, bass.ds(y0 + LATE, SEQ - LATE)], proj[:, bass.ds(y0 + SEQ, NS)]
                    tt(y_late, y_late, late_sums[a], ALU.add)
                    tt(y_smp, y_smp, smpf[:, bass.ds((i * 2 + a) * NS, NS)], ALU.add)
                dve.drain().then_inc(sem["conv_done"], 1)

            rs = part.rearrange("p (s k a) -> p s k a", a=2, k=H // 2)
            fence()
            with dve.Fori(0, NS // 2) as i_half:
                for par in range(2):
                    i = i_half * 2 + par
                    for hh in range(2):
                        dve.wait_ge(sem["scores_mm"], i * 2 + (hh + 1))
                        tt(probs[:, hh, :], pb[hh][:, 0:3 * P], cmask[:, :], ALU.add)
                        fence()
                        v.tensor_reduce(nmax[:, hh, 0:1], probs[:, hh, 0:P], X, ALU.max, negate=True)
                        v.tensor_reduce(nmax[:, hh, 1:2], probs[:, hh, P:3 * P], X, ALU.max, negate=True)\
                            .then_inc(sem["row_max"], 1)
                    conv_rounds(i_half, range(8 * par, 8 * par + 2))
                    for hh in range(2):
                        dve.wait_ge(sem["exps"], i * 2 + (hh + 1))
                        v.reciprocal(psums[:, hh, :], psums[:, hh, :])
                        fence()
                        ts(probs[:, hh, 0:P], probs[:, hh, 0:P], psums[:, hh, 0:1], None, ALU.mult)
                        ts(probs[:, hh, P:3 * P], probs[:, hh, P:3 * P], psums[:, hh, 1:2], None, ALU.mult)\
                            .then_inc(sem["probs_done"], 1)
                    conv_rounds(i_half, range(8 * par + 2, 8 * par + 5))
                    dve.wait_ge(sem["v_mm"], i + 1)
                    for half in range(2):
                        tt(own_heads[:, half * 512:(half + 1) * 512].rearrange("p (h d) -> p h d", d=HD),
                           pb[5 + half][0:H, :].rearrange("p (h d) -> p h d", d=HD),
                           ident[0:H, 8 * half:8 * half + 8].unsqueeze(2).to_broadcast([H, 8, HD]), ALU.mult)
                    dve.drain().then_inc(sem["own_masked"], 1)
                    conv_rounds(i_half, range(8 * par + 5, 8 * par + 7))
                    dve.wait_ge(sem["own_turned"], i + 1)
                    for a in range(2):
                        r = slice(64 * a, 64 * a + 64)
                        tt(attT[r, :, bass.ds(i + SEQ, 1)].rearrange("p k o -> p (k o)"), pb[7][r, 0:H // 2],
                           rs[r, bass.ds(i, 1), :, a].rearrange("p o k -> p (o k)"), ALU.mult)
                    dve.drain().then_inc(sem["smp_out"], 1)
                    conv_rounds(i_half, range(8 * par + 7, 8 * par + 8))
                    if par == 1:
                        conv_end(i_half)
            dve.wait_ge(sem["mean_mm"], 1)
            stt(y_conv, pb[6][:, 0:TOK].unsqueeze(1).to_broadcast([P, KT, TOK]), -1.0 / D, y_conv,
                ALU.mult, ALU.add).then_inc(sem["centred"], 1)
            dve.wait_ge(sem["gates"], 1)

            def branch(m, use):
                if m % 2 == 0:
                    dve.wait_ge(sem["proj_done"], 4 * use + (m // 2 + 1))
                else:
                    dve.wait_ge(free[m // 2], use + 2)

            for m in range(8):
                branch(m, SEC)
                tt(g_att[:, m, :], g_att[:, m, :], pb[m % 2][:, 0:TOK], ALU.mult).then_inc(sem["gated"], 1)
            dve.wait_ge(sem["var_mm"], 1)
            ts(pb[7][:, 0:TOK], pb[7][:, 0:TOK], 1.0 / D, EPS, ALU.mult, ALU.add).then_inc(sem["var_done"], 1)
            dve.wait_ge(sem["std_done"], 1)
            v.reciprocal(pb[7][:, 0:TOK], pb[7][:, 0:TOK])
            fence()
            tt(y_conv, y_conv, pb[7][:, 0:TOK].unsqueeze(1).to_broadcast([P, KT, TOK]), ALU.mult)\
                .then_inc(sem["normed"], 1)
            for m in range(8):
                branch(m, SEC + 1)
                tt(g_conv[:, m, :], g_conv[:, m, :], pb[m % 2][:, 0:TOK], ALU.mult)
                fence()
                tt(mT[:, m, :], g_conv[:, m, :], g_att[:, m, :], ALU.add).then_inc(sem["gated"], 1)

            def norm(x_t, n, out, turn, done):
                for a in range(2):
                    v.bn_stats(lnst[0:n, a, :], x_t[:, 512 * a:512 * (a + 1)])
                fence()
                v.bn_aggr(mv[0:n, :], lnst[0:n, :, :])
                fence()
                ts(rstd[0:n, :], mv[0:n, 1:2], EPS, None, ALU.add).then_inc(sem["row_var"], 1)
                dve.wait_ge(sem["row_std"], turn + 1)
                v.reciprocal(rstd[0:n, :], rstd[0:n, :])
                fence()
                ts(x_t, x_t, mv[0:n, 0:1], rstd[0:n, :], ALU.subtract, ALU.mult)
                fence()
                tt(x_t, x_t, ln_g[0:n, :], ALU.mult)
                fence()
                tt(out, x_t, ln_b[0:n, :], ALU.add).then_inc(sem[done], 1)

            dve.wait_ge(sem["xres_loaded"], 16 * NT)
            dve.wait_ge(sem["ln1_loaded"], 32)
            for t, (r0, n) in enumerate(TILES):
                for half in range(2):
                    dve.wait_ge(sem["mix_turned"], 2 * t + half + 1)
                    x_h = h_nat[0:n, t, 512 * half:512 * (half + 1)]
                    stt(x_h, x_h, ALPHA, pb[2 + half][0:n, :], ALU.mult, ALU.add).then_inc(sem["resid"], 1)
                fence()
                norm(h_nat[0:n, t, :], n, h_nat[0:n, t, :], t, "h_done")
            dve.wait_ge(sem["router_mm"], 1)
            dve.wait_ge(sem["late_loaded"], 48)
            dve.wait_ge(sem["pool_consts"], 2)
            for t, (r0, n) in enumerate(TILES):
                tt(logits[0:n, t, :], pb[6][0:n, t * E:(t + 1) * E], br_row[0:n, :], ALU.add)
            fence()
            for t in range(NT):
                v.max(top8[:, t, :], logits[:, t, :])
            fence()
            ts(nbig, top8[:, :, 0], -1.0, None, ALU.mult).then_inc(sem["logits_max"], 1)
            fourth = top8[:, :, TOP_K - 1:TOP_K].to_broadcast([P, NT, E])
            tt(above, logits, fourth, ALU.is_gt)
            tt(ties, logits, fourth, ALU.is_equal)
            fence()
            v.tensor_reduce(n_above, above, X, ALU.add)
            for t in range(NT):
                v.tensor_tensor_scan(slot[:, t, :], ties[:, t, :], ties[:, t, :], 0.0, ALU.add, ALU.bypass)
            fence()
            tt(slot, slot, n_above.unsqueeze(2).to_broadcast([P, NT, E]), ALU.add)
            fence()
            stt(mask, slot, float(TOP_K), ties, ALU.is_le, ALU.mult)
            fence()
            tt(mask, mask, above, ALU.add).then_inc(sem["mask_done"], 1)
            dve.wait_ge(sem["mask_done"], 1)
            dve.wait_ge(sem["exps_r"], 1)
            tt(wts, wts, mask, ALU.mult)
            fence()
            v.tensor_reduce(wsum, wts, X, ALU.add)
            fence()
            v.reciprocal(wsum, wsum)
            fence()
            tt(wts, wts, wsum.unsqueeze(2).to_broadcast([P, NT, E]), ALU.mult).then_inc(sem["weights_done"], 1)
            dve.wait_ge(sem["rank_mm"], 1)
            ranks = pb[7][:, 0:3 * E].rearrange("p (t e) -> p t e", e=E)
            stt(slot[:, 0:2, :], ranks[:, 0:2, :], 1000.0, mask[:, 0:2, :], ALU.add, ALU.mult)
            stt(slot[0:NS, 2, :], ranks[0:NS, 2, :], 1000.0, mask[0:NS, 2, :], ALU.add, ALU.mult)
            v.tensor_copy(counts, pb[7][:, 3 * E:4 * E])
            fence()
            ts(slot, slot, -1000.0, None, ALU.add)
            for c in range(4):
                ts(flags[:, c * E:(c + 1) * E], counts, float(CAP * (c + 1)), None, ALU.is_gt)
            fence()
            v.tensor_tensor_scan(prefix, flags, flags, 0.0, ALU.add, ALU.bypass)
            fence()
            ts(flags, prefix, kidx, None, ALU.is_le)
            fence()
            v.tensor_reduce(eidx[:, 0:1], flags, X, ALU.add)
            fence()
            ts(eidx[:, 1:2], eidx[:, 0:1], float(E), None, ALU.is_ge)
            for c in range(2, 5):
                fence()
                stt(eidx[:, 1:2], eidx[:, 0:1], float(E * c), eidx[:, 1:2], ALU.is_ge, ALU.add)
            fence()
            stt(eidx[:, 2:3], eidx[:, 1:2], -float(E), eidx[:, 0:1], ALU.mult, ALU.add)
            fence()
            v.tensor_copy(extra_items[:, 0:1], eidx[:, 2:3])
            ts(extra_items[:, 1:2], eidx[:, 1:2], 1.0, None, ALU.add)
            v.tensor_copy(n_extra_i[:, 0:1], prefix[0:1, 127:128])
            v.memset(n_extra_i[:, 1:2].bitcast(F32), 0.0)
            dve.drain().then_inc(sem["extras_made"], 1)
            dve.wait_ge(sem["hT_copied"], 2 * NT)
            for k in range(KT):
                dve.wait_ge(sem["bdown_mm"], k + 1)
                stt(accT[:, k, :], hT[:, k, :], ALPHA, pb[k % 2][:, 0:TOK], ALU.mult, ALU.add)\
                    .then_inc(sem["acc_init"], 1)
            dve.wait_ge(sem["acc_init"], KT)
            dve.wait_ge(sem["conv_stored"], 16 * 3)
            v.memset(out_sb, 0.0)
            v.memset(selw, 0.0)
            dve.drain().then_inc(sem["selw_ready"], 1)
            dve.sem_inc(sem["out_copied"], 2)

            dve.wait_ge(sem["extras_loaded"], 16 * 2)
            slot_f = rt[:, 480:576]
            wts_f = rt[:, 384:480]

            def item(n):
                e = dve.value_load(items[0:1, bass.ds(n, 1), 0:1].rearrange("o a b -> o (a b)"),
                                   min_val=0, max_val=E - 1)
                c = dve.value_load(items[0:1, bass.ds(n, 1), 1:2].rearrange("o a b -> o (a b)"),
                                   min_val=0, max_val=5)
                return e, c

            def one_hot(out, e, c, weighted):
                for t, (r0, n) in enumerate(TILES):
                    places = iota_f[0:n, bass.ds(c * CAP, CAP)]
                    if weighted:
                        places = places.unsqueeze(1).to_broadcast([n, 2, CAP])
                    place = slot_f[0:n, bass.ds(e + t * E, 1)]
                    if weighted:
                        last = ts(out[0:n, t, :].rearrange("p (a s) -> p a s", a=2), places, place, wts_f[0:n, bass.ds(e + t * E, 1)],
                                  ALU.is_equal, ALU.mult)
                    else:
                        last = ts(out[0:n, t, CAP:2 * CAP], places, place, None, ALU.is_equal)
                return last

            dve.wait_ge(sem["h_lo_done"], NT)
            v.tensor_copy(ident_r[:, :], ident[:, :])
            for c0 in (0, 2 * CAP):
                ts(sel[:, :, c0:c0 + CAP], ident[:, 0:CAP].unsqueeze(1).to_broadcast([P, NT, CAP]), 0.0, None,
                   ALU.mult)
            one_hot(sel, 0, 0, False)
            dve.drain().then_inc(sem["sel_ready"], 1)
            dve.wait_ge(sem["gather_mm"], 1)
            one_hot(sel, 1, 0, False).then_inc(sem["sel_ready"], 1)
            dve.wait_ge(sem["b_copied"], 1)
            n_items = dve.value_load(items[0:1, LIST - 1, 0:1], min_val=0, max_val=N_EXTRA) + E

            def split_low(place, i):
                p = pair_of(place)
                dve.wait_ge(hi_done[p], split(place, i))
                tt(w_lo[p][:, :], ring[:, 4 + slot_of(place), :], w_hi[p][:, :], ALU.subtract)\
                    .then_inc(lo_done[p], 1)

            def copy_gate_up(i, last_place):
                dve.wait_ge(pair_free[pair_of(last_place)], used(last_place, i))
                for b in (0, 1):
                    v.tensor_copy(gu_sb[:, b * 512:(b + 1) * 512], pb[b][:, :]).then_inc(sem["gu_copied"], 1)

            def gate_and_up(i, e):
                bias = [bias_gu[:, bass.ds(e * 16 + 8 * j, 8)].unsqueeze(2).to_broadcast([P, 8, CAP])
                        for j in range(2)]
                dve.wait_ge(sem["gu_turned"], i * 2)
                tt(g_buf, bank(4, KT), bias[0], ALU.add)
                tt(u_buf, bank(5, KT), bias[1], ALU.add)
                fence()
                ts(g_buf, g_buf, LIMIT, None, ALU.min).then_inc(sem["gate_ready"], 1)
                ts(u_buf, u_buf, LIMIT, -LIMIT, ALU.min, ALU.max)
                fence()
                stt(u_buf, u_buf, 1.0, g_buf, ALU.add, ALU.mult)
                fence()

            def activations(i):
                dve.wait_ge(sem["sigmoid_done"], i)
                tt(act_buf, u_buf, s_buf, ALU.mult)
                tt(act2[:, :, 0:CAP], u_buf, s_buf, ALU.mult)
                fence()
                tt(act2[:, :, CAP:2 * CAP], act_buf, act2[:, :, 0:CAP], ALU.subtract).then_inc(sem["act_ready"], 1)

            def scatter_columns(i, e, c):
                dve.wait_ge(sem["selw_turned"], i)
                one_hot(selw, e, c, True).then_inc(sem["selw_ready"], 1)

            def gather_columns(n):
                e, c = item(n)
                dve.wait_ge(sem["gather_mm"], n)
                one_hot(sel, e, c, False).then_inc(sem["sel_ready"], 1)

            def add_scattered(i, tiles):
                for k in tiles:
                    dve.wait_ge(sem["scatter_mm"], i * KT + (k + 1))
                    tt(accT[:, k, :], accT[:, k, :], pb[4 + k % 2][:, 0:TOK], ALU.add)\
                        .then_inc(sem["scatter_added"], 1)

            for place in range(4, PLACES):
                if place not in POOL_SPLITS:
                    split_low(place, 0)
            copy_gate_up(0, PLACES - 1)
            with dve.Fori(1, n_items) as i:
                e, c = item(i - 1)
                for place in (0, 1, 2):
                    split_low(place, i)
                scatter_columns(i, e, c)
                gather_columns(i + 1)
                gate_and_up(i, e)
                split_low(4, i)
                activations(i)
                split_low(5, i)
                add_scattered(i - 1, range(0, 3))
                split_low(7, i)
                add_scattered(i - 1, range(3, 6))
                split_low(8, i)
                add_scattered(i - 1, range(6, KT))
                copy_gate_up(i, KT - 1)
                split_low(10, i)
                split_low(11, i)
            e, c = item(n_items - 1)
            for place in (0, 1, 2):
                split_low(place, n_items)
            gate_and_up(n_items, e)
            activations(n_items)
            scatter_columns(n_items, e, c)
            add_scattered(n_items - 1, range(KT))
            split_low(3, n_items)
            add_scattered(n_items, range(KT))
            fence()
            dve.wait_ge(sem["ln2_loaded"], 32)
            for t, (r0, n) in enumerate(TILES):
                for half in range(2):
                    dve.wait_ge(sem["y_turned"], 2 * t + half + 1)
                    v.tensor_copy(y_nat[0:n, t, 512 * half:512 * (half + 1)], pb[half][0:n, :])\
                        .then_inc(sem["resid"], 1)
                fence()
                norm(y_nat[0:n, t, :], n, y_nat[0:n, t, :], NT + t, "y_done")


_INS = ["x_prompt", "x_sample", "cache_k", "cache_v", "cache_logf", "state_conv", "page_table",
        "w_in", "b_forget", "conv_w", "conv_b", "conv_norm_g", "conv_norm_b",
        "w_attn_proj", "w_conv_proj", "w_out", "ln1_g", "ln1_b",
        "w_router", "b_router", "w_gate_up", "b_gate_up", "w_down", "b_down", "ln2_g", "ln2_b"]
_OUTS = [(1, 256, 1024), (8, 1, 1024), (1, 1, 256, 16, 64), (1, 1, 256, 16, 64), (1, 1, 256, 16),
         (1, 1, 30, 1024), (1, 8, 1, 16, 64), (1, 8, 1, 16, 64), (1, 8, 1, 16), (1, 8, 30, 1024)]


def kernel(**inputs):
    import numpy as np
    import concourse.bacc as bacc
    from concourse.bass_utils import run_bass_kernel_spmd

    nc = bacc.Bacc("TRN2", target_bir_lowering=False, num_devices=1)
    arrays, args = {}, []
    for name in _INS:
        a = np.ascontiguousarray(inputs[name])
        arrays[f"in_{name}"] = a
        args.append(nc.dram_tensor(f"in_{name}", a.shape, mybir.dt.from_np(a.dtype), kind="ExternalInput").ap())
    for i, shape in enumerate(_OUTS):
        args.append(nc.dram_tensor(f"out_{i}", shape, F32, kind="ExternalOutput").ap())
    trunk_step(nc, *args)
    r = run_bass_kernel_spmd(nc, [arrays], core_ids=[0])
    return tuple(r.results[0][f"out_{i}"] for i in range(len(_OUTS)))
```

```python
from contextlib import ExitStack

import concourse.bass as bass
from concourse import mybir

F32 = mybir.dt.float32
F32R = mybir.dt.float32r
I32 = mybir.dt.int32
ALU = mybir.AluOpType
ACT = mybir.ActivationFunctionType
X = mybir.AxisListType.X

P = 128
NEG = -1.0e30
LIMIT = 7.0
SWIGLU_ALPHA = 1.702
EPS = 1e-5
TOP_K = 4
ALPHA = 2.0 ** 0.25
CAP = 64
POOL_SPLITS = (3, 9)
V_LOW_POOL = (0, 1, 3, 5, 7)
V_LOW_DVE = (2, 4, 6)
POOL_PAGES = (1, 3, 5, 7)

SEMAPHORES = """
x_loaded params_loaded table_loaded forget_loaded lf_loaded logf_new_loaded late_loaded ln2_loaded
extras_loaded extras_stored pool_consts x_turned x_copied params_turned params_copied smp_products
smp_conv_mm logit_mm neg_abs softplus logf_done logf_stored proj_done proj_used q_turned q_copied
q_stored qb_free kv_turned kv_copied kv_stored prodP_full prodP_free scores_done self_done
after_sums bias_mm max_part max_turned max_diag max_spread shifted sample_exps sum_part sum_spread
u_sig conv_done uout_turned uout_copied conv_stored p_parts_done prompt_read scores_mm row_stats
exps probs_done turned_mm probsT_copied oT_copied v_mm att_done v_hi_done v_low_pool v_low_dve
v_page_used pair_staged smp_out own_masked own_turned mean_mm centred squares var_mm var_done
std_done normed conv_act gates gated mixT_copied mix_turned resid row_var row_std h_done h_turned
hT_copied router_mm logits_max exps_r mask_done rank_mm weights_done wT_turned wT_copied bdown_mm
acc_init extras_made items_ready b_turned b_copied h_hi_done h_lo_done sel_ready selw_ready
gather_mm rows_copied tokens_turned xg_ready gu_copied gu_turned gate_ready sigmoid_done act_ready
selw_turned selT_copied scatter_mm scatter_added out_copied y_turned y_done y_stored
""".split()


def trunk_step(nc, x_prompt, x_sample, cache_k, cache_v, cache_logf, state_conv, page_table,
               w_in, b_forget, conv_w, conv_b, conv_norm_g, conv_norm_b,
               w_attn_proj, w_conv_proj, w_out, ln1_g, ln1_b,
               w_router, b_router, w_gate_up, b_gate_up, w_down, b_down, ln2_g, ln2_b,
               y_prompt, y_sample, k_prompt, v_prompt, logf_prompt, conv_prompt,
               k_sample, v_sample, logf_sample, conv_sample):
    _, SEQ, D = x_prompt.shape
    NS = x_sample.shape[0]
    _, _, PAGE, H, HD = cache_k.shape
    NPG = page_table.shape[1]
    W = conv_w.shape[1]
    E = w_router.shape[2]
    FF = w_down.shape[2]
    KT = D // P
    TOK = SEQ + NS
    TILES = [(0, P), (P, P), (2 * P, NS)]
    NT = len(TILES)
    SH = NS * H
    SCALE = float(HD) ** -0.5
    SEC = 7
    CH = KT * TOK
    N_EXTRA = TOK * TOP_K // CAP
    LIST = 64
    assert SEQ == 2 * P and D == 1024 and FF == D and PAGE == P and H * HD == D and NS == 8 and NPG == 8
    assert E + N_EXTRA + 2 < LIST and CAP * 4 <= TOK <= CAP * 5

    q_scratch = nc.dram_tensor("q_scratch", [NS, D], F32, kind="Internal").ap()
    extras_scratch = nc.dram_tensor("extras_scratch", [N_EXTRA + 2, 2], I32, kind="Internal").ap()
    kpages = cache_k.rearrange("o n p h d -> (o n) p (h d)")
    vpages = cache_v.rearrange("o n p h d -> (o n) p (h d)")
    fpages = cache_logf.rearrange("o n p h -> (o n) p h")
    x_rows = [x_prompt[0, 0:P, :], x_prompt[0, P:SEQ, :], x_sample.rearrange("b s d -> (b s) d")]
    y_rows = [y_prompt[0, 0:P, :], y_prompt[0, P:SEQ, :], y_sample.rearrange("b s d -> (b s) d")]
    kp_rows, vp_rows = (a.rearrange("o b s h d -> (o b s) (h d)") for a in (k_prompt, v_prompt))
    ks_rows, vs_rows = (a.rearrange("o b s h d -> (o b s) (h d)") for a in (k_sample, v_sample))
    k_rows = [kp_rows[0:P, :], kp_rows[P:SEQ, :], ks_rows]
    v_rows = [vp_rows[0:P, :], vp_rows[P:SEQ, :], vs_rows]
    lfp_rows = logf_prompt.rearrange("o b (t p) h -> p (o b t) h", p=P)
    lfs_rows = logf_sample.rearrange("o b s h -> (o b s) h")
    w_in_v = w_in.rearrange("o (k p) n -> p (o k) n", p=P)
    proj_w = [w.rearrange("o (k p) n -> p (o k) n", p=P) for w in (w_attn_proj, w_conv_proj, w_out)]
    gu_v = w_gate_up.rearrange("o e (k p) n -> (o e) k p n", p=P)
    dn_v = w_down.rearrange("o e (k t p) n -> (o e) k p t n", p=P, t=2)

    def row(par):
        return par.rearrange("o n -> (o n)").partition_broadcast(P)

    with ExitStack() as ctx:
        def sb(name, shape, dt=F32):
            return ctx.enter_context(nc.sbuf_tensor(name, shape, dt))

        sem = {n: ctx.enter_context(nc.semaphore(n)) for n in SEMAPHORES}
        full = [ctx.enter_context(nc.semaphore(f"full{i}")) for i in range(12)]
        free = [ctx.enter_context(nc.semaphore(f"free{i}")) for i in range(12)]
        hi_done = [ctx.enter_context(nc.semaphore(f"hi_done{i}")) for i in range(3)]
        lo_done = [ctx.enter_context(nc.semaphore(f"lo_done{i}")) for i in range(3)]
        pair_free = [ctx.enter_context(nc.semaphore(f"pair_free{i}")) for i in range(3)]
        qb_full = [ctx.enter_context(nc.semaphore(f"qb_full{i}")) for i in range(2)]

        places = {}

        def placed(name, shape):
            places[name] = nc.sbuf_base
            return sb(name, shape)

        def parts_at(name, shape, tensor, col):
            return nc.alloc_sbuf_tensor_at(name, shape, F32R, offset=-(-places[tensor] // 32) * 32 + 4 * col)

        ring = placed("ring", [P, 12, 2048])
        proj = placed("proj", [P, SEC * CH])
        xT = sb("xT", [P, KT, TOK])
        v_nat = placed("v_nat", [P, NT, D])
        S_smp = sb("S_smp", [P, NPG + 1, SH])
        lf = placed("lf", [P, NPG, SH])
        lf_after = placed("lf_after", [P, NPG, SH])
        asc = sb("asc", [P, 3072])
        ident = sb("ident", [P, P])
        tri = sb("tri", [P, P])
        ones_after = sb("ones_after", [P, 2 * P])
        cmask = sb("cmask", [P, 3 * P])
        smask = sb("smask", [NS, NS, H])
        blk = sb("blk", [P, 4])
        cw = sb("cw", [P, KT, W])
        cpar = sb("cpar", [P, 3 * KT])
        wf = sb("wf", [P, KT, H])
        bf_row = sb("bf_row", [P, H])
        page_ids = sb("page_ids", [1, NS * NPG], I32)
        small = placed("small", [P, 448])
        own_mask = sb("own_mask", [2 * H, H])
        items = sb("items", [1, LIST, 2], I32)
        extra_items = sb("extra_items", [P, 2], I32)
        n_extra_i = sb("n_extra_i", [1, 2], I32)

        def sec(s):
            return proj[:, s * CH:(s + 1) * CH].rearrange("p (k t) -> p k t", t=TOK)

        qT, kT, vT, u_val, u_gate, g_att, g_conv = (sec(s) for s in range(SEC))
        y_conv = u_gate
        squares = u_val
        early = ring[:, 8:12, :].rearrange("p a n -> p (a n)")
        qb = [early[:, i * D:(i + 1) * D] for i in range(2)]
        prodD = [early[:, 2 * D:3 * D], asc[:, 0:D]]
        prodP = [early[:, (3 + i) * D:(4 + i) * D] for i in range(2)]
        x_nat = early[:, 5 * D:8 * D].rearrange("p (t d) -> p t d", d=D)
        k_nat = x_nat
        SR = 4 * (W - 1)
        state_nat = v_nat[0:SR, 0:2, :]
        cw_rows = v_nat[0:SR, 2, :]
        convw_nat = asc[0:W, 0:D]
        cpar_nat = asc[0:3 * KT, D:D + P]
        self_prod = asc[0:NS, 0:D]
        q_nat = asc[0:NS, 1280:1280 + D]
        lf_cols, la_cols = (a[:, :, :].rearrange("p g n -> p (g n)") for a in (lf, lf_after))
        q_st = [asc[:, 0:256], lf_cols[:, 0:256]]
        k_st = [asc[:, 256:512], lf_cols[:, 256:512]]
        v_st = [a.rearrange("p (t c) -> p t c", c=P) for a in (asc[:, 512:768], lf_cols[:, 512:768])]
        decay = [a.rearrange("p (h a c) -> p h a c", h=2, c=P) for a in (asc[:, 768:1536], la_cols[:, 0:768])]
        p_parts = [parts_at(f"p_parts{i}", [P, NPG, 2 * H], ("lf", "lf_after")[i], 768) for i in range(2)]
        p_new = parts_at("p_new", [P, 2, 2 * H], "small", 384)
        v_new = parts_at("v_new", [P, 2, D], "ring", 2048)
        v_hi = parts_at("v_hi", [P, 4, D], "ring", 2048 * 2)
        v_lo = parts_at("v_lo", [P, 16, D], "ring", 2048 * 4)
        probs = asc[:, 1536:2304].rearrange("p (h c) -> p h c", h=2)
        probsT = asc[:, 2304:3072].rearrange("p (h c) -> p h c", h=2)
        attT = xT
        own_heads = proj[0:2 * H, 2 * CH:2 * CH + D]
        LATE = (W + 1) // 2
        late_sums = [proj[:, 2 * CH + D + a * SEQ:2 * CH + D + a * SEQ + SEQ - LATE] for a in range(3)]
        h_nat = proj[:, 0:3 * D].rearrange("p (t d) -> p t d", d=D)
        ln_g, ln_b = proj[:, 3 * D:4 * D], proj[:, 4 * D:5 * D]
        out_sb = proj[:, 5 * D:6 * D]
        mixT, hT, mT, accT = u_val, u_gate, g_conv, xT
        m0, m1 = 3 * CH, 4 * CH
        g_buf, u_buf, s_buf, act_buf = (
            proj[:, m0 + 512 * i:m0 + 512 * (i + 1)].rearrange("p (k s) -> p k s", s=CAP) for i in range(4))
        gu_sb = proj[:, m1:m1 + 2 * FF]
        selT = lf_cols[:, 0:TOK]
        selw = lf_cols[:, TOK:TOK + 2 * NT * CAP].rearrange("p (t s) -> p t s", s=2 * CAP)
        x_rows_r = parts_at("x_rows_r", [P, D], "proj", 0)
        sel = parts_at("sel", [P, NT, 3 * CAP], "proj", D)
        ident_r = parts_at("ident_r", [P, P], "proj", D + 9 * CAP)
        act2 = parts_at("act2", [P, KT, 2 * CAP], "lf_after", 0)
        h_hi = parts_at("h_hi", [P, NT, D], "v_nat", 0)
        h_lo = parts_at("h_lo", [P, NT, D], "proj", 5 * CH)
        xg = parts_at("xg", [P, KT, 2 * CAP], "proj", 5 * CH + 3 * D)
        w_hi = [parts_at(f"w_hi{i}", [P, 2048], "ring", 2048 * (10, 0, 2)[i]) for i in range(3)]
        w_lo = [parts_at(f"w_lo{i}", [P, 2048], "ring", 2048 * (11, 1, 3)[i]) for i in range(3)]
        y_nat = proj[:, 5 * CH:5 * CH + 3 * D].rearrange("p (t d) -> p t d", d=D)
        bd_nat = S_smp[0:E, 0:NPG, :].rearrange("p g n -> p (g n)")
        uout_p, uout_s = (a.rearrange("p g n -> p (g n)") for a in (lf[0:W - 1], lf_after[0:NS]))
        rt = asc[:, 0:904]
        logits, above, ties, mask, wts, slot = (
            rt[:, 96 * i:96 * (i + 1)].rearrange("p (t e) -> p t e", e=E) for i in range(6))
        top8 = rt[:, 576:600].rearrange("p (t e) -> p t e", e=8)
        n_above, wsum, nbig = rt[:, 600:603], rt[:, 603:606], rt[:, 606:609]
        counts = rt[:, 609:641]
        flags, prefix = rt[:, 641:769], rt[:, 769:897]
        eidx = rt[:, 897:903]
        iota_f = asc[:, 904:1288]
        wcT = asc[0:E, 1288:1288 + TOK]
        tri_s = asc[:, 1552:1680]
        router_w = asc[:, 1680:1936].rearrange("p (k e) -> p k e", e=E)
        bgu_nat = asc[:, 1936:2448].rearrange("p (a b) -> p a b", b=P)
        bias_gu = asc[:, 2448:2960]
        br_row = asc[:, 2960:2992]
        sum_halves = asc[:, 2992:3056]
        zf, na, logf = (small[:, 48 * i:48 * (i + 1)].rearrange("p (t h) -> p t h", h=H) for i in range(3))
        self_s = small[0:NS, 144:160]
        nmax = small[:, 160:164].rearrange("p (h a) -> p h a", h=2)
        psums = small[:, 164:168].rearrange("p (h a) -> p h a", h=2)
        smax = small[:, 168:169]
        lnst = small[:, 170:182].rearrange("p (a b) -> p a b", b=6)
        mv, rstd = small[:, 182:184], small[:, 184:185]
        kidx = small[:, 186:187]
        smp_conv = small[:, 192:256].rearrange("p (c b) -> p c b", b=NS)
        part = small[:, 256:384]
        logf_row = sb("logf_row", [1, SH])
        o_smp = sb("o_smp", [P, NS + 1, H // 2])

        onesm, after = ones_after[:, 0:P], ones_after[:, P:2 * P]
        pb = [ctx.enter_context(nc.psum_tensor(f"pb{i}", [P, 512], F32)) for i in range(8)]
        block = ctx.enter_context(nc.Block())

        def bank(i, k):
            return pb[i][:, :].rearrange("p (k n) -> p k n", k=k)

        K_USES, V_USES = NS, NS // 2

        def value_page(par, g):
            return ring[:, 4 + 4 * par + g // 2, (g % 2) * D:(g % 2 + 1) * D]

        def v_low_count(s, g):
            if g in V_LOW_DVE:
                return "v_low_dve", s * len(V_LOW_DVE) + (V_LOW_DVE.index(g) + 1)
            return "v_low_pool", s * len(V_LOW_POOL) + (V_LOW_POOL.index(g) + 2)

        PLACES, SLOTS = 12, 6
        LATE_LOADS = NT + 6

        def slot_of(place):
            return (place + 2) % SLOTS

        def pair_of(place):
            return (place + 2) % 3

        def loaded(place, i):
            s = slot_of(place)
            before = 32 * (K_USES + V_USES) if s < 4 else 32 * V_USES
            return i * 32 + (before + 16 * ((place - 4) // SLOTS + 1))

        def split(place, i):
            return i * 4 + ((place - 4) // 3 + 1)

        def used(place, i):
            return split(place, i) + 1

        @block.sync
        def _(sp):
            def load_w(src, use, c):
                sp.wait_ge(free[c], use + 1)
                sp.dma_start(ring[:, c, :].rearrange("p (k n) -> p k n", k=KT), src).then_inc(full[c], 16)

            def w_in_cols(start, c):
                return w_in_v[:, :, bass.ds(start + 256 * c, 256)]

            def load_pages(pages, s, r, buf, uses):
                sp.wait_ge(free[buf], uses + 1)
                for g in (2 * r, 2 * r + 1):
                    pid = sp.value_load(page_ids[0:1, bass.ds(s * NPG + g, 1)], min_val=0,
                                        max_val=cache_k.shape[1] - 1)
                    sp.dma_start(ring[:, buf, (g % 2) * D:(g % 2 + 1) * D],
                                 pages[bass.ds(pid, 1), :, :].rearrange("o p n -> (o p) n"))\
                        .then_inc(full[buf], 16)
                    if pages is kpages:
                        sp.dma_start(lf[:, g, bass.ds(s * H, H)],
                                     fpages[bass.ds(pid, 1), :, :].rearrange("o p n -> (o p) n"))\
                            .then_inc(sem["lf_loaded"], 16)

            def load_query(s, par):
                sp.wait_ge(sem["qb_free"], s + 1)
                sp.dma_start(qb[par], q_scratch[bass.ds(s, 1), :].rearrange("o n -> (o n)")
                             .partition_broadcast(P)).then_inc(qb_full[par], 16)

            for b in range(12):
                sp.sem_inc(free[b], 1)
            for t, (r0, n) in enumerate(TILES):
                sp.dma_start(x_nat[0:n, t, :], x_rows[t]).then_inc(sem["x_loaded"], 16)
            load_w(w_in_cols(0, 0), 0, 0)
            sp.dma_start(page_ids[:, :], page_table.rearrange("a (o b) -> o (a b)", o=1))\
                .then_inc(sem["table_loaded"], 16)
            for c in range(1, 4):
                load_w(w_in_cols(0, c), 0, c)
            sp.dma_start(wf[:, :, :], w_in_v[:, :, 3 * D:3 * D + H]).then_inc(sem["forget_loaded"], 16)
            sp.dma_start(bf_row[:, :], row(b_forget)).then_inc(sem["forget_loaded"], 16)
            sp.dma_start(convw_nat, conv_w[0, :, :]).then_inc(sem["params_loaded"], 16)
            for i, par in enumerate((conv_b, conv_norm_g, conv_norm_b)):
                sp.dma_start(cpar_nat[i * KT:(i + 1) * KT, :], par.rearrange("o (k p) -> (o k) p", p=P))\
                    .then_inc(sem["params_loaded"], 16)
            for i in range(2):
                sp.dma_start(state_nat[:, i, :],
                             state_conv[0, 4 * i:4 * i + 4, :, :].rearrange("b w c -> (b w) c"))\
                    .then_inc(sem["params_loaded"], 16)
            for i in range(4):
                sp.dma_start(cw_rows[i * (W - 1):(i + 1) * (W - 1), :], conv_w[0, 0:W - 1, :])\
                    .then_inc(sem["params_loaded"], 16)
            sp.wait_ge(sem["table_loaded"], 16)
            for r in range(4):
                load_pages(kpages, 0, r, 4 + r, 0)
            for c in range(4):
                load_w(w_in_cols(D, c), 1, c)
            sp.wait_ge(sem["q_stored"], 16)
            load_query(0, 0)

            def keys_and_section(s, start, use):
                for c in range(4):
                    if c % 2 == 0:
                        load_query(s + c // 2, 1 - c // 2)
                    for r in (2 * c % 4, 2 * c % 4 + 1):
                        load_pages(kpages, s + c // 2, r, 4 + r, s + c // 2)
                    load_w(w_in_cols(start, c), use, c)

            keys_and_section(1, 2 * D, 2)
            with sp.Fori(0, 2) as i:
                keys_and_section(i * 2 + 3, i * D + (3 * D + H), i + 3)
            load_query(NS - 1, 1)
            for r in range(4):
                load_pages(kpages, NS - 1, r, 4 + r, NS - 1)
                load_w(w_in_cols(5 * D + H, r), 5, r)
            for c in range(4):
                load_w(w_in_cols(6 * D + H, c), 6, c)
            sp.wait_ge(sem["logf_stored"], 32)
            sp.dma_start(logf_row[:, :], lfs_rows.rearrange("s (o h) -> o s h", o=1))\
                .then_inc(sem["logf_new_loaded"], 16)
            sp.dma_start(conv_sample[0, :, 0:W - 2, :], state_conv[0, :, 1:W - 1, :])\
                .then_inc(sem["conv_stored"], 16)
            for r in range(4):
                load_pages(vpages, 0, r, 4 + r, K_USES)
            sp.wait_ge(sem["scores_done"], NS)
            sp.wait_ge(sem["self_done"], 1)
            sp.wait_ge(sem["kv_stored"], 16 * 2 * NT)
            for r in range(4):
                load_pages(vpages, 1, r, 8 + r, 0)
            load_w(proj_w[0][:, :, 0:256], SEC, 0)
            with sp.Fori(1, NS // 2) as i:
                for par in range(2):
                    for r in range(4):
                        load_pages(vpages, i * 2 + par, r, 4 + 4 * par + r,
                                   i + K_USES if par == 0 else i)
            sp.wait_ge(sem["v_mm"], NS)
            for c in range(1, 4):
                load_w(proj_w[0][:, :, 256 * c:256 * (c + 1)], SEC, c)

            def load_chunk(src, place, i, first=False):
                s = slot_of(place)
                if first:
                    sp.wait_ge(free[4 + s], (K_USES + V_USES if s < 4 else V_USES) + 1)
                else:
                    sp.wait_ge(lo_done[pair_of(place)], split(place, i) - 2)
                sp.dma_start(ring[:, 4 + s, :].rearrange("p (t n) -> p t n", t=2), src).then_inc(full[4 + s], 16)

            def gate_up(e, c):
                return gu_v[bass.ds(e, 1), c, :, :].rearrange("o p (t n) -> (o p) t n", t=2)

            def load_down(e, place, i):
                for k in range(4):
                    load_chunk(dn_v[bass.ds(e, 1), k, :, :, :].rearrange("o p t n -> (o p) t n"), place + k, i)

            sp.wait_ge(sem["att_done"], 1)
            sp.wait_ge(sem["own_turned"], NS + 1)
            for t, (r0, n) in enumerate(TILES):
                sp.dma_start(h_nat[0:n, t, :], x_rows[t]).then_inc(sem["late_loaded"], 16)
            sp.dma_start(router_w, w_router.rearrange("o (k p) e -> p (o k) e", p=P))\
                .then_inc(sem["late_loaded"], 16)
            sp.dma_start(br_row, row(b_router)).then_inc(sem["late_loaded"], 16)
            sp.dma_start(bgu_nat, b_gate_up.rearrange("o (a e) (j p) -> (o e j) a p", p=P, a=4))\
                .then_inc(sem["late_loaded"], 16)
            sp.dma_start(bd_nat, b_down[0, :, :]).then_inc(sem["late_loaded"], 16)
            for line, par in ((ln_g, ln1_g), (ln_b, ln1_b)):
                sp.dma_start(line, row(par)).then_inc(sem["late_loaded"], 16)
            for c in range(SLOTS):
                load_chunk(gate_up(0, c), 4 + c, 0, first=True)
            for w in (1, 2):
                for c in range(4):
                    load_w(proj_w[w][:, :, 256 * c:256 * (c + 1)], SEC + w, c)
            for c in range(SLOTS, KT):
                load_chunk(gate_up(0, c), 4 + c, 0)
            with sp.Fori(1, E) as e:
                for c in range(KT):
                    load_chunk(gate_up(e, c), c, e)
                load_down(e - 1, KT, e)
            sp.wait_ge(sem["items_ready"], 1)
            n_extra = sp.value_load(items[0:1, LIST - 1, 0:1], min_val=0, max_val=N_EXTRA)
            n_items = n_extra + E

            def expert_of(i):
                return sp.value_load(items[0:1, bass.ds(i, 1), 0:1].rearrange("o a b -> o (a b)"),
                                     min_val=0, max_val=E - 1)

            with sp.If(n_extra):
                with sp.Fori(E, n_items) as i:
                    e = expert_of(i)
                    for c in range(KT):
                        load_chunk(gate_up(e, c), c, i)
                    load_down(expert_of(i - 1), KT, i)
            load_down(expert_of(n_items - 1), 0, n_items)
            for t, (r0, n) in enumerate(TILES):
                sp.wait_ge(sem["y_done"], t + 1)
                sp.dma_start(y_rows[t], y_nat[0:n, t, :]).then_inc(sem["y_stored"], 16)
            sp.wait_ge(sem["y_stored"], 16 * NT)
            sp.wait_ge(sem["conv_stored"], 16 * 3)

        @block.gpsimd
        def _(pool):
            def fence():
                pool.drain()

            nc.gpsimd.memset(ident[:, :], 1.0)
            nc.gpsimd.memset(tri[:, :], 1.0)
            nc.gpsimd.memset(ones_after[:, :], 1.0)
            nc.gpsimd.memset(cmask[:, :], 0.0)
            nc.gpsimd.memset(smask[:, :, :], 0.0)
            nc.gpsimd.memset(blk[:, :], 1.0)
            nc.gpsimd.memset(small[:, :], 0.0)
            nc.gpsimd.memset(S_smp[:, NPG, :], NEG)
            fence()
            nc.gpsimd.affine_select(out=ident[:, :], in_=ident[:, :], pattern=[[-1, P]], base=0,
                                    channel_multiplier=1, compare_op=ALU.is_equal, fill=0.0)
            nc.gpsimd.affine_select(out=tri[:, :], in_=tri[:, :], pattern=[[1, P]], base=0,
                                    channel_multiplier=-1, compare_op=ALU.is_ge, fill=0.0)
            nc.gpsimd.affine_select(out=after, in_=after, pattern=[[-1, P]], base=0,
                                    channel_multiplier=1, compare_op=ALU.is_gt, fill=0.0)
            for a in (0, 2):
                m = cmask[:, a * P:(a + 1) * P]
                nc.gpsimd.affine_select(out=m, in_=m, pattern=[[-1, P]], base=0,
                                        channel_multiplier=1, compare_op=ALU.is_ge, fill=NEG)
            nc.gpsimd.affine_select(out=smask[:, :, :], in_=smask[:, :, :], pattern=[[-1, NS], [0, H]], base=0,
                                    channel_multiplier=1, compare_op=ALU.is_equal, fill=NEG)
            nc.gpsimd.affine_select(out=blk[:, :], in_=blk[:, :], pattern=[[1 - W, 4]], base=0,
                                    channel_multiplier=1, compare_op=ALU.is_ge, fill=0.0)
            fence()
            nc.gpsimd.affine_select(out=blk[:, :], in_=blk[:, :], pattern=[[W - 1, 4]], base=W - 2,
                                    channel_multiplier=-1, compare_op=ALU.is_ge, fill=0.0)
            nc.gpsimd.iota(items[:, :, :], pattern=[[1, LIST], [0, 2]], base=0, channel_multiplier=0)
            fence()
            nc.gpsimd.tensor_tensor(own_mask[:, :], ident[0:2 * H, 0:H], ident[0:2 * H, H:2 * H], ALU.add)
            nc.gpsimd.memset(items[:, :, 1:2].bitcast(F32), 0.0)
            nc.gpsimd.iota(kidx, pattern=[[0, 1]], base=0, channel_multiplier=1,
                           allow_small_or_imprecise_dtypes=True)
            pool.drain().then_inc(sem["pool_consts"], 1)

            def key_products(s, par, n_par):
                pool.wait_ge(qb_full[par], n_par * 16 + 16)
                for j, g in enumerate(POOL_PAGES):
                    pool.wait_ge(full[4 + g // 2], s * 32 + 32)
                    pool.wait_ge(sem["prodP_free"], s * len(POOL_PAGES) + (j + 1))
                    nc.gpsimd.tensor_tensor(prodP[j % 2], ring[:, 4 + g // 2, (g % 2) * D:(g % 2 + 1) * D],
                                            qb[par], ALU.mult).then_inc(sem["prodP_full"], 1)

            with pool.Fori(0, NS // 2) as i:
                for par in range(2):
                    key_products(i * 2 + par, par, i)

            pool.wait_ge(sem["bias_mm"], 1)

            def probs_parts(i, par):
                pool.wait_ge(sem["sample_exps"], 1)
                pool.wait_ge(sem["prompt_read"], i + 1)
                p_pages, p_last = S_smp[:, 0:NPG, bass.ds(i * H, H)], S_smp[:, NPG, bass.ds(i * H, H)]
                nc.gpsimd.tensor_copy(p_parts[par][:, :, 0:H], p_pages)
                nc.gpsimd.tensor_copy(p_new[:, par, 0:H], p_last)
                fence()
                nc.gpsimd.tensor_tensor(p_parts[par][:, :, H:2 * H], p_pages, p_parts[par][:, :, 0:H], ALU.subtract)
                nc.gpsimd.tensor_tensor(p_new[:, par, H:2 * H], p_last, p_new[:, par, 0:H], ALU.subtract)
                pool.drain().then_inc(sem["p_parts_done"], 1)

            def values_low(s, par, pages):
                for g in pages:
                    pool.wait_ge(sem["v_hi_done"], s * NPG + (g + 2))
                    nc.gpsimd.tensor_tensor(v_lo[:, NPG * par + g, :], value_page(par, g), v_hi[:, g % 4, :],
                                            ALU.subtract).then_inc(sem["v_low_pool"], 1)

            def sequence_parts(i, par, last=False):
                values_low(i, par, [g for g in V_LOW_POOL if g < 4])
                if not last:
                    probs_parts(i + 1, 1 - par)
                values_low(i, par, [g for g in V_LOW_POOL if g >= 4])

            pool.wait_ge(sem["v_hi_done"], 1)
            nc.gpsimd.tensor_tensor(v_new[0:NS, 1, :], v_nat[0:NS, 2, :], v_new[0:NS, 0, :], ALU.subtract)\
                .then_inc(sem["v_low_pool"], 1)
            probs_parts(0, 0)
            with pool.Fori(0, NS // 2 - 1) as i:
                for par in range(2):
                    sequence_parts(i * 2 + par, par)
            sequence_parts(NS - 2, 0)
            sequence_parts(NS - 1, 1, last=True)
            pool.wait_ge(sem["att_done"], 1)
            pool.wait_ge(sem["v_mm"], NS)
            nc.gpsimd.iota(iota_f, pattern=[[1, 6 * CAP]], base=0, channel_multiplier=0,
                           allow_small_or_imprecise_dtypes=True)
            nc.gpsimd.memset(rt[:, :], 0.0)
            nc.gpsimd.tensor_tensor(tri_s, tri[:, :], ident[:, :], ALU.subtract)
            nc.gpsimd.tensor_tensor(sum_halves, ident[:, 0:CAP], ident[:, CAP:2 * CAP], ALU.add)
            pool.drain().then_inc(sem["pool_consts"], 1)

            def split_low(place, i):
                p = pair_of(place)
                pool.wait_ge(hi_done[p], split(place, i))
                nc.gpsimd.tensor_tensor(w_lo[p][:, :], ring[:, 4 + slot_of(place), :], w_hi[p][:, :],
                                        ALU.subtract).then_inc(lo_done[p], 1)

            for t, (r0, n) in enumerate(TILES):
                if t < 2:
                    split_low(4 + t, 0)
                pool.wait_ge(sem["h_hi_done"], t + 1)
                nc.gpsimd.tensor_tensor(h_lo[0:n, t, :], h_nat[0:n, t, :], h_hi[0:n, t, :], ALU.subtract)\
                    .then_inc(sem["h_lo_done"], 1)
            pool.wait_ge(sem["h_turned"], 2 * NT)
            pool.wait_ge(sem["h_lo_done"], NT)
            nc.gpsimd.tensor_copy(ident_r[:, :], ident[:, :])
            for t in range(NT):
                for c0 in (0, 2 * CAP):
                    nc.gpsimd.tensor_scalar(sel[:, t, c0:c0 + CAP], ident[:, 0:CAP], 0.0, None, ALU.mult)
            pool.drain().then_inc(sem["h_lo_done"], 1)
            split_low(6, 0)
            split_low(POOL_SPLITS[1], 0)
            pool.wait_ge(sem["items_ready"], 1)
            n_items = pool.value_load(items[0:1, LIST - 1, 0:1], min_val=0, max_val=N_EXTRA) + E
            with pool.Fori(1, n_items) as i:
                for place in POOL_SPLITS:
                    split_low(place, i)

        @block.tensor
        def _(pe):
            mm, tr = nc.tensor.matmul, nc.tensor.transpose

            pe.wait_ge(sem["pool_consts"], 1)
            pe.wait_ge(sem["x_loaded"], 16 * NT)
            for t, (r0, n) in enumerate(TILES):
                for half in range(2):
                    b = 2 * t + half
                    if b >= 2:
                        pe.wait_ge(sem["x_copied"], b - 1)
                    for k in range(4):
                        c0 = (4 * half + k) * P
                        last = tr(bank(2 + b % 2, 4)[:, k, 0:n], x_nat[0:n, t, c0:c0 + P], ident[0:n, 0:n])
                    last.then_inc(sem["x_turned"], 1)

            def project(src, slots_done, used, tiles0, tiles=range(8)):
                for m in tiles:
                    c = m // 2
                    if m % 2 == 0:
                        pe.wait_ge(full[c], slots_done * 16 + 16)
                    pe.wait_ge(used, tiles0 + (m + 1))
                    w = ring[:, c, :].rearrange("p (k n) -> p k n", k=KT)
                    for k in range(KT):
                        last = mm(pb[m % 2][:, 0:TOK], w[:, k, (m % 2) * P:(m % 2 + 1) * P], src[:, k, :],
                                  start=(k == 0), stop=(k == KT - 1))
                    last.then_inc(sem["proj_done"] if m % 2 == 0 else free[c], 1)

            def section(s, tiles=range(8)):
                project(xT, s, sem["proj_used"], s * 8, tiles)

            pe.wait_ge(sem["x_copied"], 2 * NT)
            section(0)
            pe.wait_ge(sem["proj_used"], 2 + 8)
            for k in range(KT):
                last = tr(bank(2 + k // 4, 4)[0:NS, k % 4, :], qT[:, k, SEQ:TOK], ident[:, :])
            last.then_inc(sem["q_turned"], 1)
            pe.wait_ge(sem["params_loaded"], 16 * 10)
            for k in range(KT):
                tr(pb[5][:, k * W:(k + 1) * W], convw_nat[:, k * P:(k + 1) * P], ident[0:W, 0:W])
            tr(pb[5][:, 256:256 + 3 * KT], cpar_nat, ident[0:3 * KT, 0:3 * KT])\
                .then_inc(sem["params_turned"], 1)
            pe.wait_ge(sem["smp_products"], 1)
            for k in range(KT):
                for i in range(2):
                    c0 = k * NS + 4 * i
                    last = mm(pb[7][:, c0:c0 + 4], state_nat[:, i, k * P:(k + 1) * P], blk[0:SR, :],
                              start=True, stop=True)
            last.then_inc(sem["smp_conv_mm"], 1)
            pe.wait_ge(sem["forget_loaded"], 32)
            pe.wait_ge(sem["x_copied"], 2 * NT)
            for t, (r0, n) in enumerate(TILES):
                for k in range(KT):
                    last = mm(pb[6][0:n, t * H:(t + 1) * H], xT[:, k, r0:r0 + n], wf[:, k, :],
                              start=(k == 0), stop=(k == KT - 1))
            last.then_inc(sem["logit_mm"], 1)
            with pe.Fori(1, 3) as s:
                section(s)
            pe.wait_ge(sem["proj_used"], 2 + 24)
            pe.wait_ge(sem["q_copied"], 2)
            for i, src in enumerate((kT, vT)):
                for t, (r0, n) in enumerate(TILES):
                    for half in range(2):
                        b = 6 * i + 2 * t + half
                        if b >= 2:
                            pe.wait_ge(sem["kv_copied"], b - 1)
                        for k in range(4):
                            last = tr(bank(2 + b % 2, 4)[0:n, k, :], src[:, 4 * half + k, r0:r0 + n], ident[:, :])
                        last.then_inc(sem["kv_turned"], 1)
            with pe.Fori(3, SEC - 1) as s:
                section(s)
            section(SEC - 1, range(0, 2))
            pe.wait_ge(sem["after_sums"], 1)
            for half in range(2):
                a, b = 4 * half, 4 * half + 4
                mm(pb[4 + half][:, :], after, lf[:, a:b, :], start=True, stop=False)
                last = mm(pb[4 + half][:, :], onesm, lf_after[:, a:b, :], start=False, stop=True)
            last.then_inc(sem["bias_mm"], 1)
            section(SEC - 1, range(2, 4))
            pe.wait_ge(sem["max_part"], 1)
            pe.wait_ge(sem["kv_copied"], 4 * NT)
            tr(pb[2][:, 0:SH], part, ident[:, :]).then_inc(sem["max_turned"], 1)
            section(SEC - 1, range(4, 6))
            pe.wait_ge(sem["max_diag"], 1)
            mm(pb[3][:, 0:SH], onesm, part, start=True, stop=True).then_inc(sem["max_spread"], 1)
            section(SEC - 1, range(6, 8))

            def values(s, par, pages):
                for g in pages:
                    if g == NPG:
                        lhs = p_new[0:NS, par, :]
                        parts = (v_new[0:NS, 0, :], v_new[0:NS, 1, :])
                    else:
                        lhs = p_parts[par][:, g, :]
                        parts = (v_hi[:, g % 4, :], v_lo[:, NPG * par + g, :])
                    for k, v in enumerate(parts):
                        if k == 0:
                            pe.wait_ge(sem["v_hi_done"], s * NPG + (g + 2) if g < NPG else 1)
                        elif g < NPG:
                            name, count = v_low_count(s, g)
                            pe.wait_ge(sem[name], count)
                        else:
                            pe.wait_ge(sem["v_low_pool"], 1)
                        for half in range(2):
                            last = mm(pb[5 + half][0:2 * H, :], lhs, v[:, half * 512:(half + 1) * 512],
                                      start=(g == 0 and k == 0), stop=(g == NPG and k == 1))
                        if k == 0 and g < NPG:
                            last.then_inc(sem["v_page_used"], 1)
                        elif g % 2 == 1:
                            last.then_inc(free[4 + 4 * par + g // 2], 1)
                        elif k == 1 and g == NPG:
                            last.then_inc(sem["v_mm"], 1)

            def turn_own_heads(s):
                pe.wait_ge(sem["own_masked"], s + 1)
                pe.wait_ge(sem["smp_out"], s + 1)
                for hp in range(H // 2):
                    last = mm(pb[7][:, hp:hp + 1], own_heads[:, hp * P:(hp + 1) * P], onesm[0:2 * H, 0:1],
                              start=True, stop=True)
                last.then_inc(sem["own_turned"], 1)

            def head_pair(i, j):
                par = j % 2
                pe.wait_ge(sem["pair_staged"], i + 1)
                for hh in range(2):
                    pe.wait_ge(sem["probs_done"], i * 2 + (hh + 1))
                    r = slice(64 * hh, 64 * hh + 64)
                    s0, s1 = pb[hh][:, 0:P], pb[hh][:, P:3 * P]
                    mm(s0, q_st[par][r, 0:P], k_st[par][r, 0:P], start=True, stop=False)
                    mm(s0, decay[par][:, hh, 0, :], after, start=False, stop=True)
                    mm(s1, q_st[par][r, P:2 * P], k_st[par][r, :], start=True, stop=False)
                    mm(s1[:, 0:P], decay[par][:, hh, 1, :], after, start=False, stop=False)
                    mm(s1, decay[par][:, hh, 2, :], ones_after[:, :], start=False, stop=True)\
                        .then_inc(sem["scores_mm"], 1)
                pe.wait_ge(sem["own_masked"], i + 1)
                pe.wait_ge(sem["p_parts_done"], i + 1)
                values(i, par, range(0, 4))
                turn_own_heads(i)
                values(i, par, range(4, 6))
                for hh in range(2):
                    pe.wait_ge(sem["probs_done"], i * 2 + (hh + 3))
                    for c in range(3):
                        last = tr(bank(2 + hh, 4)[:, c, :], probs[:, hh, c * P:(c + 1) * P], ident[:, :])
                    last.then_inc(sem["turned_mm"], 1)
                values(i, par, range(6, NPG + 1))
                pe.wait_ge(sem["oT_copied"], i + 1)
                for hh in range(2):
                    pe.wait_ge(sem["probsT_copied"], i * 2 + (hh + 1))
                    o = pb[4][64 * hh:64 * hh + 64, 0:SEQ]
                    v = v_st[par][:, :, 64 * hh:64 * hh + 64]
                    mm(o, v[:, 0, :], probsT[:, hh, 0:2 * P], start=True, stop=False)
                    last = mm(o[:, P:2 * P], v[:, 1, :], probsT[:, hh, 2 * P:3 * P], start=False, stop=True)
                last.then_inc(sem["prompt_read"], 1)

            pe.wait_ge(sem["proj_used"], 2 + 8 * SEC)
            with pe.Fori(0, NS // 4) as i_four:
                for j in range(4):
                    head_pair(i_four * 4 + j, j)
            for j, (a, b) in enumerate(((SEQ - (W - 1), SEQ), (SEQ, TOK))):
                if j == 1:
                    pe.wait_ge(sem["uout_copied"], 2)
                for k in range(KT):
                    last = tr(bank(2 + k // 4, 4)[0:b - a, k % 4, :], u_val[:, k, a:b], ident[:, :])
                last.then_inc(sem["uout_turned"], 1)
            pe.wait_ge(sem["sum_part"], 1)
            mm(pb[0][:, 0:SH], onesm, part, start=True, stop=True).then_inc(sem["sum_spread"], 1)
            turn_own_heads(NS)
            pe.wait_ge(sem["conv_done"], 3)
            for k in range(KT):
                last = mm(pb[6][:, 0:TOK], onesm, y_conv[:, k, :], start=(k == 0), stop=(k == KT - 1))
            last.then_inc(sem["mean_mm"], 1)
            pe.wait_ge(sem["att_done"], 1)
            pe.wait_ge(sem["smp_out"], NS + 2)
            project(attT, SEC, sem["gated"], 0, range(0, 2))
            pe.wait_ge(sem["squares"], 1)
            for k in range(KT):
                last = mm(pb[7][:, 0:TOK], onesm, squares[:, k, :], start=(k == 0), stop=(k == KT - 1))
            last.then_inc(sem["var_mm"], 1)
            project(attT, SEC, sem["gated"], 0, range(2, 8))
            pe.wait_ge(sem["late_loaded"], 16 * LATE_LOADS)
            for a in range(4):
                last = tr(bank(4, 4)[:, a, :], bgu_nat[:, a, :], ident[:, :])
            last.then_inc(sem["b_turned"], 1)
            pe.wait_ge(sem["conv_act"], 1)
            project(y_conv, SEC + 1, sem["gated"], 8)
            pe.wait_ge(sem["gated"], 2 + 16)
            project(mT, SEC + 2, sem["mixT_copied"], 0)
            for t, (r0, n) in enumerate(TILES):
                for half in range(2):
                    b = 2 * t + half
                    pe.wait_ge(sem["mixT_copied"], 2 + 8)
                    if b >= 2:
                        pe.wait_ge(sem["resid"], b - 1)
                    else:
                        pe.wait_ge(sem["uout_copied"], 4)
                    for k in range(4):
                        last = tr(bank(2 + b % 2, 4)[0:n, k, :], mixT[:, 4 * half + k, r0:r0 + n], ident[:, :])
                    last.then_inc(sem["mix_turned"], 1)
            for t, (r0, n) in enumerate(TILES):
                pe.wait_ge(sem["h_done"], t + 1)
                pe.wait_ge(sem["b_copied"], 1)
                for half in range(2):
                    b = 2 * t + half
                    if b >= 2:
                        pe.wait_ge(sem["hT_copied"], b - 1)
                    for k in range(4):
                        c0 = (4 * half + k) * P
                        last = tr(bank(4 + b % 2, 4)[:, k, 0:n], h_nat[0:n, t, c0:c0 + P], ident[0:n, 0:n])
                    last.then_inc(sem["h_turned"], 1)
                pe.wait_ge(sem["hT_copied"], 2 * t + 2)
                for k in range(KT):
                    last = mm(pb[6][0:n, t * E:(t + 1) * E], hT[:, k, r0:r0 + n], router_w[:, k, :],
                              start=(k == 0), stop=(k == KT - 1))
            last.then_inc(sem["router_mm"], 1)
            pe.wait_ge(sem["mask_done"], 1)
            pe.wait_ge(sem["pool_consts"], 2)
            for t, (r0, n) in enumerate(TILES):
                for j in range(t + 1):
                    rows = TILES[j][1]
                    lhs = tri_s if j == t else onesm
                    last = mm(pb[7][0:n, t * E:(t + 1) * E], lhs[0:rows, 0:n], mask[0:rows, j, :],
                              start=(j == 0), stop=(j == t))
            for j, (_, rows) in enumerate(TILES):
                last = mm(pb[7][:, 3 * E:4 * E], onesm[0:rows, :], mask[0:rows, j, :],
                          start=(j == 0), stop=(j == NT - 1))
            last.then_inc(sem["rank_mm"], 1)

            def gather(n):
                pe.wait_ge(sem["sel_ready"], n + 1)
                for half in range(2):
                    for h_part, c0 in ((h_hi, CAP), (h_lo, 0)):
                        for t, (r0, rows) in enumerate(TILES):
                            last = mm(pb[6 + half][:, :], sel[0:rows, t, c0:c0 + 2 * CAP],
                                      h_part[0:rows, t, half * 512:(half + 1) * 512],
                                      start=h_part is h_hi and t == 0, stop=h_part is h_lo and t == NT - 1)
                last.then_inc(sem["gather_mm"], 1)

            def turn_tokens(n):
                pe.wait_ge(sem["rows_copied"], n * 2 + 2)
                for k in range(KT):
                    last = mm(bank(6 + k // 4, 4)[:, k % 4, :], x_rows_r[:, k * P:(k + 1) * P], ident_r[:, :],
                              start=True, stop=True)
                last.then_inc(sem["tokens_turned"], 1)

            def scatter(n, tiles):
                for k in tiles:
                    pe.wait_ge(sem["scatter_added"], n * KT + (k + 1))
                    mm(pb[4 + k % 2][:, 0:TOK], out_sb[:, k * P:(k + 1) * P], selT, start=True, stop=True)\
                        .then_inc(sem["scatter_mm"], 1)

            def turn_columns(n):
                pe.wait_ge(sem["selw_ready"], n + 1)
                for t, (r0, rows) in enumerate(TILES):
                    last = tr(pb[6][:, r0:r0 + rows], selw[0:rows, t, :], ident[0:rows, 0:rows])
                last.then_inc(sem["selw_turned"], 1)

            def gate_up(i, c, place):
                p = pair_of(place)
                for w, done in ((w_hi[p], hi_done[p]), (w_lo[p], lo_done[p])):
                    pe.wait_ge(done, split(place, i))
                    for b in range(4):
                        last = mm(pb[b][:, :], xg[:, c, :], w[:, b * 512:(b + 1) * 512],
                                  start=c == 0 and w is w_hi[p], stop=c == KT - 1 and w is w_lo[p])
                last.then_inc(pair_free[p], 1)

            def turn_gate_up(half):
                for j in range(KT):
                    last = mm(bank(4 + half, KT)[:, j, :], gu_sb[:, (half * KT + j) * P:(half * KT + j + 1) * P],
                              sum_halves, start=True, stop=True)
                last.then_inc(sem["gu_turned"], 1)

            def down(i, place):
                pe.wait_ge(sem["act_ready"], i)
                for k in range(4):
                    p = pair_of(place + k)
                    for w, done in ((w_hi[p], hi_done[p]), (w_lo[p], lo_done[p])):
                        pe.wait_ge(done, split(place + k, i))
                        for j in range(4):
                            last = mm(pb[4 + j % 2][:, :], act2[:, 2 * k + j // 2, :], w[:, j * 512:(j + 1) * 512],
                                      start=k == 0 and w is w_hi[p] and j < 2,
                                      stop=k == 3 and w is w_lo[p] and j >= 2)
                    last.then_inc(pair_free[p], 1)

            pe.wait_ge(sem["weights_done"], 1)
            for t, (r0, n) in enumerate(TILES):
                last = tr(pb[2][0:E, r0:r0 + n], wts[0:n, t, :], ident[0:n, 0:n])
            last.then_inc(sem["wT_turned"], 1)
            gather(0)
            turn_tokens(0)
            pe.wait_ge(sem["wT_copied"], 1)
            pe.wait_ge(sem["late_loaded"], 16 * LATE_LOADS)
            for k in range(KT):
                if k >= 2:
                    pe.wait_ge(sem["acc_init"], k - 1)
                mm(pb[4 + k % 2][:, 0:TOK], bd_nat[:, k * P:(k + 1) * P], wcT, start=True, stop=True)\
                    .then_inc(sem["bdown_mm"], 1)
            pe.wait_ge(sem["acc_init"], KT)
            pe.wait_ge(sem["xg_ready"], 2)
            for c in range(KT):
                gate_up(0, c, 4 + c)
            gather(1)
            turn_tokens(1)
            pe.wait_ge(sem["items_ready"], 1)
            n_items = pe.value_load(items[0:1, LIST - 1, 0:1], min_val=0, max_val=N_EXTRA) + E
            with pe.Fori(1, n_items) as i:
                pe.wait_ge(sem["xg_ready"], i * 2 + 2)
                turn_columns(i - 1)
                pe.wait_ge(sem["gu_copied"], i * 4)
                gate_up(i, 0, 0)
                pe.wait_ge(sem["out_copied"], i * 2)
                turn_gate_up(0)
                gate_up(i, 1, 1)
                turn_gate_up(1)
                gate_up(i, 2, 2)
                gate_up(i, 3, 3)
                pe.wait_ge(sem["selT_copied"], i)
                gather(i + 1)
                gate_up(i, 4, 4)
                gate_up(i, 5, 5)
                turn_tokens(i + 1)
                pe.wait_ge(sem["gate_ready"], i)
                scatter(i - 1, range(0, 3))
                gate_up(i, 6, 6)
                scatter(i - 1, range(3, 6))
                gate_up(i, 7, 7)
                scatter(i - 1, range(6, 8))
                pe.wait_ge(sem["scatter_added"], i * KT + 2)
                down(i, KT)
            pe.wait_ge(sem["gu_copied"], n_items * 4)
            pe.wait_ge(sem["out_copied"], n_items * 2)
            turn_gate_up(0)
            turn_gate_up(1)
            pe.wait_ge(sem["xg_ready"], n_items * 2 + 2)
            turn_columns(n_items - 1)
            pe.wait_ge(sem["gate_ready"], n_items)
            pe.wait_ge(sem["selT_copied"], n_items)
            scatter(n_items - 1, range(KT))
            pe.wait_ge(sem["scatter_added"], n_items * KT + 2)
            down(n_items, 0)
            pe.wait_ge(sem["out_copied"], n_items * 2 + 2)
            turn_columns(n_items)
            pe.wait_ge(sem["selT_copied"], n_items + 1)
            scatter(n_items, range(KT))
            for t, (r0, n) in enumerate(TILES):
                pe.wait_ge(sem["scatter_added"], n_items * KT + (KT + 2))
                for k in range(KT):
                    last = tr(bank(2 * t + k // 4, 4)[0:n, k % 4, :], accT[:, k, r0:r0 + n], ident[:, :])
                last.then_inc(sem["y_turned"], 1)

        @block.scalar
        def _(act):
            def copy(out, in_, scale=None):
                if scale is None:
                    return nc.scalar.copy(out, in_)
                return nc.scalar.activation(out, in_, ACT.Copy, scale=scale)

            act.sem_inc(sem["proj_used"], 2)
            act.sem_inc(sem["mixT_copied"], 2)
            act.sem_inc(sem["oT_copied"], 1)
            act.sem_inc(sem["v_page_used"], 4)
            for t, (r0, n) in enumerate(TILES):
                for half in range(2):
                    b = 2 * t + half
                    act.wait_ge(sem["x_turned"], b + 1)
                    copy(xT[:, 4 * half:4 * half + 4, r0:r0 + n], bank(2 + b % 2, 4)[:, :, 0:n])\
                        .then_inc(sem["x_copied"], 1)

            def store_section(s, scale=None, tiles=range(8)):
                for m in tiles:
                    if m % 2 == 0:
                        act.wait_ge(sem["proj_done"], s * 4 + (m // 2 + 1))
                    else:
                        act.wait_ge(free[m // 2], s + 2)
                    copy(proj[:, bass.ds(s * CH + m * TOK, TOK)], pb[m % 2][:, 0:TOK], scale)\
                        .then_inc(sem["proj_used"], 1)

            store_section(0, SCALE)
            act.wait_ge(sem["q_turned"], 1)
            for half in range(2):
                copy(q_nat[:, 512 * half:512 * (half + 1)], pb[2 + half][0:NS, :]).then_inc(sem["q_copied"], 1)
            act.wait_ge(sem["q_copied"], 2)
            act.dma_start(q_scratch, q_nat).then_inc(sem["q_stored"], 16)
            act.wait_ge(sem["params_turned"], 1)
            copy(cw[:, :, :], pb[5][:, 0:KT * W].rearrange("p (k w) -> p k w", w=W))
            copy(cpar[:, :], pb[5][:, 256:256 + 3 * KT]).then_inc(sem["params_copied"], 1)
            act.wait_ge(sem["smp_conv_mm"], 1)
            act.wait_ge(sem["pool_consts"], 1)
            copy(smp_conv, pb[7][:, 0:KT * NS].rearrange("p (c b) -> p c b", b=NS))
            act.wait_ge(sem["neg_abs"], 1)
            nc.scalar.activation(na, na, ACT.Exp)
            act.drain()
            nc.scalar.activation(na, na, ACT.Ln, bias=1.0).then_inc(sem["softplus"], 1)
            act.wait_ge(sem["logf_done"], 1)
            act.dma_start(lfp_rows, logf[:, 0:2, :]).then_inc(sem["logf_stored"], 16)
            act.dma_start(lfs_rows, logf[0:NS, 2, :]).then_inc(sem["logf_stored"], 16)
            with act.Fori(1, 3) as s:
                store_section(s)
            for i, (dst, rows) in enumerate(((k_nat, k_rows), (v_nat, v_rows))):
                for t, (r0, n) in enumerate(TILES):
                    for half in range(2):
                        b = 6 * i + 2 * t + half
                        act.wait_ge(sem["kv_turned"], b + 1)
                        copy(dst[0:n, t, 512 * half:512 * (half + 1)], pb[2 + b % 2][0:n, :])\
                            .then_inc(sem["kv_copied"], 1)
                    act.wait_ge(sem["kv_copied"], 6 * i + 2 * t + 2)
                    act.dma_start(rows[t], dst[0:n, t, :]).then_inc(sem["kv_stored"], 16)
            with act.Fori(3, 5) as s:
                store_section(s)
            act.wait_ge(sem["proj_used"], 2 + 40)
            nc.scalar.activation(u_gate, u_gate, ACT.Sigmoid).then_inc(sem["u_sig"], 1)
            store_section(5)
            store_section(6, tiles=range(0, 6))

            def stage(i, par):
                copy(q_st[par], proj[:, bass.ds(i * TOK, SEQ)])
                copy(k_st[par], proj[:, bass.ds(i * TOK + CH, SEQ)])
                copy(v_st[par], v_nat[:, 0:2, bass.ds(i * P, P)])
                for hh in range(2):
                    for a, (rows, t) in enumerate(((tri[:, :], 0), (onesm, 0), (tri[:, :], 1))):
                        last = copy(decay[par][:, hh, a, :], rows, logf[:, t, bass.ds(i * 2 + hh, 1)])
                last.then_inc(sem["pair_staged"], 1)

            act.wait_ge(sem["kv_copied"], 4 * NT)
            act.wait_ge(sem["q_stored"], 16)
            act.wait_ge(sem["self_done"], 1)
            act.wait_ge(sem["bias_mm"], 1)
            stage(0, 0)
            stage(1, 1)
            act.wait_ge(sem["shifted"], 1)
            nc.scalar.activation(S_smp[:, :, :], S_smp[:, :, :], ACT.Exp).then_inc(sem["sample_exps"], 1)
            store_section(6, tiles=range(6, 8))

            def values_high(s, par, n_par, pages, before=None):
                for g in pages:
                    buf = 4 + 4 * par + g // 2
                    if g % 2 == 0:
                        act.wait_ge(full[buf], n_par * 32 + (32 * K_USES + 32 if par == 0 else 32))
                    act.wait_ge(sem["v_page_used"], s * NPG + (g + 1))
                    if g >= 4 or before is not None:
                        of, old = (s, g - 4) if g >= 4 else (before, g + 4)
                        name, count = v_low_count(of, old)
                        act.wait_ge(sem[name], count)
                    copy(v_hi[:, g % 4, :], value_page(par, g)).then_inc(sem["v_hi_done"], 1)

            def softmax_pair(i, par, n_par, staging=True, ahead=True):
                for hh in range(2):
                    act.wait_ge(sem["row_stats"], i * 3 + (hh + 1))
                    for j, (a, b) in enumerate(((0, P), (P, 3 * P))):
                        last = nc.scalar.activation(probs[:, hh, a:b], probs[:, hh, a:b], ACT.Exp,
                                                    bias=nmax[:, hh, j:j + 1], accum_out=psums[:, hh, j:j + 1])
                    last.then_inc(sem["exps"], 1)
                values_high(i, par, n_par, range(4, 6))
                act.wait_ge(sem["row_stats"], i * 3 + 3)
                for hh in range(2):
                    copy(probs[:, hh, 0:P], probs[:, hh, 0:P], psums[:, hh, 0:1])
                    copy(probs[:, hh, P:3 * P], probs[:, hh, P:3 * P], psums[:, hh, 1:2])\
                        .then_inc(sem["probs_done"], 1)
                values_high(i, par, n_par, range(6, NPG))
                for hh in range(2):
                    act.wait_ge(sem["turned_mm"], i * 2 + (hh + 1))
                    copy(probsT[:, hh, :], pb[2 + hh][:, 0:3 * P]).then_inc(sem["probsT_copied"], 1)
                if ahead:
                    values_high(i + 1, 1 - par, n_par + par, range(0, 2), before=i)
                act.wait_ge(sem["prompt_read"], i + 3)
                copy(attT[:, bass.ds(i, 1), 0:SEQ].rearrange("p a t -> p (a t)"), pb[4][:, 0:SEQ])\
                    .then_inc(sem["oT_copied"], 1)
                if ahead:
                    values_high(i + 1, 1 - par, n_par + par, range(2, 4), before=i)
                if staging:
                    stage(i + 2, par)

            act.wait_ge(free[1], SEC + 1)
            copy(v_new[0:NS, 0, :], v_nat[0:NS, 2, :]).then_inc(sem["v_hi_done"], 1)
            act.wait_ge(free[2], SEC + 1)
            act.wait_ge(free[3], SEC + 1)
            values_high(0, 0, 0, range(0, 4))
            with act.Fori(0, NS // 2 - 1) as i:
                for par in range(2):
                    softmax_pair(i * 2 + par, par, i)
            softmax_pair(NS - 2, 0, NS // 2 - 1, staging=False)
            softmax_pair(NS - 1, 1, NS // 2 - 1, staging=False, ahead=False)
            act.drain().then_inc(sem["att_done"], 1)
            for j, dst in enumerate((uout_p, uout_s)):
                act.wait_ge(sem["uout_turned"], j + 1)
                for half in range(2):
                    copy(dst[:, 512 * half:512 * (half + 1)], pb[2 + half][0:dst.shape[0], :])\
                        .then_inc(sem["uout_copied"], 1)
                act.wait_ge(sem["uout_copied"], 2 * j + 2)
                act.dma_start(conv_prompt[0, 0, :, :] if j == 0 else conv_sample[0, :, W - 2, :], dst)\
                    .then_inc(sem["conv_stored"], 16)
            act.wait_ge(sem["proj_used"], 2 + 56)
            for g in (g_att, g_conv):
                last = nc.scalar.activation(g, g, ACT.Sigmoid)
            last.then_inc(sem["gates"], 1)
            act.wait_ge(sem["centred"], 1)
            nc.scalar.activation(squares, y_conv, ACT.Square).then_inc(sem["squares"], 1)
            act.wait_ge(sem["var_done"], 1)
            nc.scalar.activation(pb[7][:, 0:TOK], pb[7][:, 0:TOK], ACT.Sqrt).then_inc(sem["std_done"], 1)
            act.wait_ge(sem["normed"], 1)
            for k in range(KT):
                last = nc.scalar.activation(y_conv[:, k, :], y_conv[:, k, :], ACT.Silu,
                                            bias=cpar[:, 2 * KT + k:2 * KT + k + 1],
                                            scale=cpar[:, KT + k:KT + k + 1])
            last.then_inc(sem["conv_act"], 1)
            act.wait_ge(sem["b_turned"], 1)
            copy(bias_gu, pb[4][:, :]).then_inc(sem["b_copied"], 1)
            for m in range(8):
                if m % 2 == 0:
                    act.wait_ge(sem["proj_done"], 4 * (SEC + 2) + (m // 2 + 1))
                else:
                    act.wait_ge(free[m // 2], SEC + 4)
                copy(mixT[:, m, :], pb[m % 2][:, 0:TOK]).then_inc(sem["mixT_copied"], 1)

            def std(turn):
                act.wait_ge(sem["row_var"], turn + 1)
                nc.scalar.activation(rstd, rstd, ACT.Sqrt).then_inc(sem["row_std"], 1)

            def hT_copy(t):
                n, r0 = TILES[t][1], TILES[t][0]
                for half in range(2):
                    b = 2 * t + half
                    act.wait_ge(sem["h_turned"], b + 1)
                    copy(hT[:, 4 * half:4 * half + 4, r0:r0 + n], bank(4 + b % 2, 4)[:, :, 0:n])\
                        .then_inc(sem["hT_copied"], 1)

            def h_high(t):
                n = TILES[t][1]
                act.wait_ge(sem["h_done"], t + 1)
                copy(h_hi[0:n, t, :], h_nat[0:n, t, :]).then_inc(sem["h_hi_done"], 1)

            def copy_rows(n):
                act.wait_ge(sem["gather_mm"], n + 1)
                for half in range(2):
                    copy(x_rows_r[:, 512 * half:512 * (half + 1)], pb[6 + half][:, :])\
                        .then_inc(sem["rows_copied"], 1)

            def gathered(n):
                act.wait_ge(sem["tokens_turned"], n + 1)
                for half in range(2):
                    copy(xg[:, 4 * half:4 * half + 4, :], bank(6 + half, 4)).then_inc(sem["xg_ready"], 1)

            def split_high(place, i):
                p, s = pair_of(place), slot_of(place)
                act.wait_ge(full[4 + s], loaded(place, i))
                act.wait_ge(pair_free[p], used(place, i) - 1)
                copy(w_hi[p][:, :], ring[:, 4 + s, :]).then_inc(hi_done[p], 1)

            act.wait_ge(sem["kv_stored"], 16 * 2 * NT)
            act.wait_ge(sem["v_mm"], NS)
            for c in range(4):
                act.wait_ge(free[c], SEC + 4)
            for t in range(NT):
                split_high(4 + t, 0)
                std(t)
                if t:
                    hT_copy(t - 1)
                    h_high(t - 1)
            hT_copy(NT - 1)
            h_high(NT - 1)
            act.wait_ge(sem["logits_max"], 1)
            for t in range(NT):
                last = nc.scalar.activation(wts[:, t, :], logits[:, t, :], ACT.Exp, bias=nbig[:, t:t + 1])
            last.then_inc(sem["exps_r"], 1)
            act.wait_ge(sem["wT_turned"], 1)
            copy(wcT, pb[2][0:E, 0:TOK]).then_inc(sem["wT_copied"], 1)

            def copy_out(i, last_place):
                act.wait_ge(pair_free[pair_of(last_place)], used(last_place, i))
                for n in range(2):
                    copy(out_sb[:, n * 512:(n + 1) * 512], pb[4 + n][:, :]).then_inc(sem["out_copied"], 1)

            def copy_gate_up(i, last_place):
                act.wait_ge(pair_free[pair_of(last_place)], used(last_place, i))
                for b in (2, 3):
                    copy(gu_sb[:, b * 512:(b + 1) * 512], pb[b][:, :]).then_inc(sem["gu_copied"], 1)

            def sigmoid(i):
                act.wait_ge(sem["gate_ready"], i)
                nc.scalar.activation(s_buf, g_buf, ACT.Sigmoid, scale=SWIGLU_ALPHA).then_inc(sem["sigmoid_done"], 1)

            def copy_columns(n):
                act.wait_ge(sem["selw_turned"], n + 1)
                copy(selT, pb[6][:, 0:TOK]).then_inc(sem["selT_copied"], 1)

            copy_rows(0)
            gathered(0)
            act.wait_ge(sem["extras_made"], 1)
            act.dma_start(extras_scratch, extra_items[0:N_EXTRA + 2, :]).then_inc(sem["extras_stored"], 16)
            act.dma_start(items[0:1, LIST - 1, :], n_extra_i[:, :]).then_inc(sem["extras_loaded"], 16)
            act.wait_ge(sem["h_done"], NT)
            for line, par in ((ln_g, ln2_g), (ln_b, ln2_b)):
                act.dma_start(line, row(par)).then_inc(sem["ln2_loaded"], 16)
            act.wait_ge(sem["extras_stored"], 16)
            act.dma_start(items[0:1, E:E + N_EXTRA + 2, :], extras_scratch.unsqueeze(0))\
                .then_inc(sem["extras_loaded"], 16)
            split_high(7, 0)
            split_high(8, 0)
            act.wait_ge(sem["extras_loaded"], 32)
            act.sem_inc(sem["items_ready"], 1)
            for place in (9, 10, 11):
                split_high(place, 0)
            n_items = act.value_load(items[0:1, LIST - 1, 0:1], min_val=0, max_val=N_EXTRA) + E
            copy_gate_up(0, PLACES - 1)
            copy_rows(1)
            gathered(1)
            for place in (0, 1, 2):
                split_high(place, 1)
            with act.Fori(1, n_items) as i:
                copy_columns(i - 1)
                split_high(3, i)
                split_high(4, i)
                sigmoid(i)
                split_high(5, i)
                copy_rows(i + 1)
                for place in range(6, KT + 2):
                    split_high(place, i)
                copy_gate_up(i, KT - 1)
                gathered(i + 1)
                split_high(10, i)
                split_high(11, i)
                split_high(0, i + 1)
                split_high(1, i + 1)
                copy_out(i, PLACES - 1)
                split_high(2, i + 1)
            copy_columns(n_items - 1)
            sigmoid(n_items)
            split_high(3, n_items)
            copy_out(n_items, 3)
            copy_columns(n_items)
            for t in range(NT):
                std(NT + t)

        @block.vector
        def _(dve):
            v = nc.vector
            stt, tt, ts = v.scalar_tensor_tensor, v.tensor_tensor, v.tensor_scalar

            def fence():
                dve.drain()

            dve.sem_inc(sem["qb_free"], 1)
            dve.sem_inc(sem["qb_free"], 1)
            dve.sem_inc(sem["prodP_free"], 2)
            dve.sem_inc(sem["probs_done"], 2)
            dve.sem_inc(sem["gated"], 2)
            dve.sem_inc(sem["scatter_added"], 2)
            for p in range(3):
                dve.sem_inc(pair_free[p], 1)
            dve.sem_inc(sem["prompt_read"], 2)
            dve.sem_inc(sem["smp_out"], 1)
            dve.wait_ge(sem["params_loaded"], 16 * 10)
            for i in range(2):
                tt(state_nat[:, i, :], state_nat[:, i, :], cw_rows, ALU.mult)
            dve.drain().then_inc(sem["smp_products"], 1)
            dve.wait_ge(sem["pool_consts"], 1)
            dve.wait_ge(sem["logit_mm"], 1)
            dve.wait_ge(sem["forget_loaded"], 32)
            tt(zf[:, 0:2, :], pb[6][:, 0:2 * H].rearrange("p (t h) -> p t h", h=H),
               bf_row[:, :].unsqueeze(1).to_broadcast([P, 2, H]), ALU.add)
            tt(zf[0:NS, 2, :], pb[6][0:NS, 2 * H:3 * H], bf_row[0:NS, :], ALU.add)
            fence()
            stt(na, zf, -1.0, zf, ALU.mult, ALU.min).then_inc(sem["neg_abs"], 1)
            dve.wait_ge(sem["softplus"], 1)
            stt(logf, zf, 0.0, na, ALU.min, ALU.subtract).then_inc(sem["logf_done"], 1)

            def add_products(s, g, prod):
                return v.tensor_reduce(S_smp[:, g, bass.ds(s * H, H)], prod.rearrange("p (h d) -> p h d", h=H),
                                       X, ALU.add)

            def pool_page(s, r):
                dve.wait_ge(sem["prodP_full"], s * 4 + (r + 1))
                add_products(s, 2 * r + 1, prodP[r % 2]).then_inc(sem["prodP_free"], 1)
                dve.drain().then_inc(free[4 + r], 1)

            def key_scores(s, par, n_par):
                dve.wait_ge(qb_full[par], n_par * 16 + 16)
                for r in range(4):
                    dve.wait_ge(full[4 + r], s * 32 + 32)
                    tt(prodD[r % 2], ring[:, 4 + r, 0:D], qb[par], ALU.mult)
                    if r:
                        pool_page(s, r - 1)
                    else:
                        fence()
                    add_products(s, 2 * r, prodD[r % 2])
                pool_page(s, 3)
                dve.drain().then_inc(sem["scores_done"], 1)
                dve.sem_inc(sem["qb_free"], 1)

            dve.wait_ge(sem["params_copied"], 1)
            with dve.Fori(0, NS // 2) as i:
                for par in range(2):
                    key_scores(i * 2 + par, par, i)
            dve.wait_ge(sem["kv_copied"], 2 * NT)
            tt(self_prod, q_nat, k_nat[0:NS, 2, :], ALU.mult)
            fence()
            v.tensor_reduce(self_s, self_prod.rearrange("p (h d) -> p h d", h=H), X, ALU.add)
            fence()
            tt(S_smp[0:NS, NPG, :].rearrange("p (s h) -> p s h", h=H), smask[:, :, :],
               self_s.unsqueeze(1).to_broadcast([NS, NS, H]), ALU.add).then_inc(sem["self_done"], 1)
            dve.wait_ge(sem["lf_loaded"], 16 * NS * NPG)
            v.memset(lf_after[:, NPG - 1, :], 0.0)
            for g in range(NPG - 2, -1, -1):
                fence()
                tt(lf_after[:, g, :], lf_after[:, g + 1, :], lf[:, g + 1, :], ALU.add)
            fence()
            dve.wait_ge(sem["logf_new_loaded"], 16)
            tt(lf_after[0:1, :, :], lf_after[0:1, :, :], logf_row[:, :].unsqueeze(1).to_broadcast([1, NPG, SH]),
               ALU.add).then_inc(sem["after_sums"], 1)
            dve.wait_ge(sem["u_sig"], 1)
            tt(u_val, u_val, u_gate, ALU.mult)
            fence()
            dve.wait_ge(sem["kv_copied"], 4 * NT)
            v.memset(own_heads, 0.0)
            cwf = cw[:, :, :].rearrange("p k w -> p (k w)")
            smpf = small[:, 192:256]

            def conv_rounds(tile, n_tiles, rounds):
                for d in rounds:
                    for a in range(n_tiles):
                        u0, w0 = (tile + a) * TOK + 3 * CH, (tile + a) * W + (W - 1)
                        late, w_d = late_sums[a], cwf[:, bass.ds(w0 - d, 1)]
                        if d == 0:
                            ts(proj[:, bass.ds(u0 + CH, TOK)], proj[:, bass.ds(u0, TOK)], w_d,
                               cpar[:, bass.ds(tile + a, 1)], ALU.mult, ALU.add)
                        else:
                            acc = proj[:, bass.ds(u0 + (CH + d), SEQ - d)]
                            stt(acc, proj[:, bass.ds(u0, SEQ - d)], w_d, acc, ALU.mult, ALU.add)
                        if LATE + d < W:
                            w_l, n = cwf[:, bass.ds(w0 - LATE - d, 1)], SEQ - LATE - d
                            if d == 0:
                                ts(late, proj[:, bass.ds(u0, n)], w_l, None, ALU.mult)
                            else:
                                stt(late[:, d:], proj[:, bass.ds(u0, n)], w_l, late[:, d:], ALU.mult, ALU.add)
                    fence()

            def conv_end(tile, n_tiles):
                for a in range(n_tiles):
                    y0 = (tile + a) * TOK + 4 * CH
                    y_late, y_smp = proj[:, bass.ds(y0 + LATE, SEQ - LATE)], proj[:, bass.ds(y0 + SEQ, NS)]
                    tt(y_late, y_late, late_sums[a], ALU.add)
                    tt(y_smp, y_smp, smpf[:, bass.ds((tile + a) * NS, NS)], ALU.add)
                dve.drain().then_inc(sem["conv_done"], 1)

            conv_rounds(0, 2, range(0, 3))
            dve.wait_ge(sem["bias_mm"], 1)
            for half in range(2):
                sl = S_smp[:, 4 * half:4 * half + 4, :]
                tt(sl, sl, bank(4 + half, 4), ALU.add)
            fence()
            v.tensor_reduce(part, S_smp[:, :, :].rearrange("p g n -> p n g"), X, ALU.max)\
                .then_inc(sem["max_part"], 1)
            conv_rounds(0, 2, range(3, 7))
            dve.wait_ge(sem["max_turned"], 1)
            v.tensor_reduce(smax, pb[2][:, 0:SH], X, ALU.max)
            fence()
            ts(part, ident[:, :], smax, None, ALU.mult).then_inc(sem["max_diag"], 1)
            conv_rounds(0, 2, range(7, 12))
            dve.wait_ge(sem["max_spread"], 1)
            tt(S_smp[:, :, :], S_smp[:, :, :], pb[3][:, 0:SH].unsqueeze(1).to_broadcast([P, NPG + 1, SH]),
               ALU.subtract).then_inc(sem["shifted"], 1)
            conv_rounds(0, 2, range(12, 16))
            conv_end(0, 2)
            dve.wait_ge(sem["sample_exps"], 1)
            v.tensor_reduce(part, S_smp[:, :, :].rearrange("p g n -> p n g"), X, ALU.add)\
                .then_inc(sem["sum_part"], 1)
            fence()
            dve.sem_inc(sem["own_masked"], 1)
            with dve.Fori(0, NS // 4) as i_four:
                for j in range(4):
                    i = i_four * 4 + j

                    def values_low(g):
                        dve.wait_ge(sem["v_hi_done"], i * NPG + (g + 2))
                        tt(v_lo[:, NPG * (j % 2) + g, :], value_page(j % 2, g), v_hi[:, g % 4, :],
                           ALU.subtract).then_inc(sem["v_low_dve"], 1)

                    values_low(V_LOW_DVE[0])
                    for hh in range(2):
                        dve.wait_ge(sem["scores_mm"], i * 2 + (hh + 1))
                        tt(probs[:, hh, :], pb[hh][:, 0:3 * P], cmask[:, :], ALU.add)
                        fence()
                        v.tensor_reduce(nmax[:, hh, 0:1], probs[:, hh, 0:P], X, ALU.max, negate=True)
                        v.tensor_reduce(nmax[:, hh, 1:2], probs[:, hh, P:3 * P], X, ALU.max, negate=True)\
                            .then_inc(sem["row_stats"], 1)
                    conv_rounds(i_four * 3 + 2, 3, range(4 * j, 4 * j + 1))
                    dve.wait_ge(sem["exps"], i * 2 + 2)
                    v.reciprocal(psums, psums).then_inc(sem["row_stats"], 1)
                    values_low(V_LOW_DVE[1])
                    conv_rounds(i_four * 3 + 2, 3, range(4 * j + 1, 4 * j + 2))
                    for g in V_LOW_DVE[2:]:
                        values_low(g)
                    conv_rounds(i_four * 3 + 2, 3, range(4 * j + 2, 4 * j + 4))
                    if j == 3:
                        conv_end(i_four * 3 + 2, 3)
                    dve.wait_ge(sem["own_turned"], i + 1)
                    v.tensor_copy(o_smp[:, bass.ds(i, 1), :].rearrange("p o k -> p (o k)"), pb[7][:, 0:H // 2])\
                        .then_inc(sem["smp_out"], 1)
                    dve.wait_ge(sem["v_mm"], i + 1)
                    for half in range(2):
                        last = tt(own_heads[:, half * 512:(half + 1) * 512].rearrange("p (h d) -> p h d", d=HD),
                                  pb[5 + half][0:2 * H, :].rearrange("p (h d) -> p h d", d=HD),
                                  own_mask[:, 8 * half:8 * half + 8].unsqueeze(2).to_broadcast([2 * H, 8, HD]),
                                  ALU.mult)
                    dve.drain().then_inc(sem["own_masked"], 1)
            dve.wait_ge(sem["sum_spread"], 1)
            v.reciprocal(part, pb[0][:, 0:SH])
            dve.wait_ge(sem["own_turned"], NS + 1)
            v.tensor_copy(o_smp[:, NS, :], pb[7][:, 0:H // 2])
            fence()
            rs = part.rearrange("p (s k a) -> p k s a", a=2, k=H // 2)
            for a in range(2):
                r = slice(64 * a, 64 * a + 64)
                tt(attT[r, :, SEQ:TOK], o_smp[r, 1:NS + 1, :].rearrange("p s k -> p k s"), rs[r, :, :, a], ALU.mult)
            dve.drain().then_inc(sem["smp_out"], 1)
            dve.wait_ge(sem["mean_mm"], 1)
            stt(y_conv, pb[6][:, 0:TOK].unsqueeze(1).to_broadcast([P, KT, TOK]), -1.0 / D, y_conv,
                ALU.mult, ALU.add).then_inc(sem["centred"], 1)
            dve.wait_ge(sem["gates"], 1)

            def branch(m, use):
                if m % 2 == 0:
                    dve.wait_ge(sem["proj_done"], 4 * use + (m // 2 + 1))
                else:
                    dve.wait_ge(free[m // 2], use + 2)

            def attention_gate(tiles):
                for m in tiles:
                    branch(m, SEC)
                    tt(g_att[:, m, :], g_att[:, m, :], pb[m % 2][:, 0:TOK], ALU.mult).then_inc(sem["gated"], 1)

            attention_gate(range(0, 2))
            dve.wait_ge(sem["var_mm"], 1)
            ts(pb[7][:, 0:TOK], pb[7][:, 0:TOK], 1.0 / D, EPS, ALU.mult, ALU.add).then_inc(sem["var_done"], 1)
            dve.wait_ge(sem["std_done"], 1)
            v.reciprocal(pb[7][:, 0:TOK], pb[7][:, 0:TOK])
            fence()
            tt(y_conv, y_conv, pb[7][:, 0:TOK].unsqueeze(1).to_broadcast([P, KT, TOK]), ALU.mult)\
                .then_inc(sem["normed"], 1)
            attention_gate(range(2, 8))
            for m in range(8):
                branch(m, SEC + 1)
                tt(g_conv[:, m, :], g_conv[:, m, :], pb[m % 2][:, 0:TOK], ALU.mult)
                fence()
                tt(mT[:, m, :], g_conv[:, m, :], g_att[:, m, :], ALU.add).then_inc(sem["gated"], 1)

            def norm(halves, n, out, turn, done):
                for a in range(2):
                    v.bn_stats(lnst[0:n, a, :], halves[a])
                fence()
                v.bn_aggr(mv[0:n, :], lnst[0:n, :, :])
                fence()
                ts(rstd[0:n, :], mv[0:n, 1:2], EPS, None, ALU.add).then_inc(sem["row_var"], 1)
                for a in range(2):
                    c = slice(512 * a, 512 * (a + 1))
                    stt(out[:, c], halves[a], mv[0:n, 0:1], ln_g[0:n, c], ALU.subtract, ALU.mult)
                dve.wait_ge(sem["row_std"], turn + 1)
                v.reciprocal(rstd[0:n, :], rstd[0:n, :])
                fence()
                stt(out, out, rstd[0:n, :], ln_b[0:n, :], ALU.mult, ALU.add).then_inc(sem[done], 1)

            dve.wait_ge(sem["late_loaded"], 16 * LATE_LOADS)
            for t, (r0, n) in enumerate(TILES):
                for half in range(2):
                    dve.wait_ge(sem["mix_turned"], 2 * t + half + 1)
                    x_h = h_nat[0:n, t, 512 * half:512 * (half + 1)]
                    stt(x_h, x_h, ALPHA, pb[2 + half][0:n, :], ALU.mult, ALU.add).then_inc(sem["resid"], 1)
                fence()
                h_t = h_nat[0:n, t, :]
                norm([h_t[:, 0:512], h_t[:, 512:D]], n, h_t, t, "h_done")
            dve.wait_ge(sem["router_mm"], 1)
            dve.wait_ge(sem["late_loaded"], 16 * LATE_LOADS)
            dve.wait_ge(sem["pool_consts"], 2)
            for t, (r0, n) in enumerate(TILES):
                tt(logits[0:n, t, :], pb[6][0:n, t * E:(t + 1) * E], br_row[0:n, :], ALU.add)
            fence()
            for t in range(NT):
                v.max(top8[:, t, :], logits[:, t, :])
            fence()
            ts(nbig, top8[:, :, 0], -1.0, None, ALU.mult).then_inc(sem["logits_max"], 1)
            fourth = top8[:, :, TOP_K - 1:TOP_K].to_broadcast([P, NT, E])
            tt(above, logits, fourth, ALU.is_gt)
            tt(ties, logits, fourth, ALU.is_equal)
            fence()
            v.tensor_reduce(n_above, above, X, ALU.add)
            for t in range(NT):
                v.tensor_tensor_scan(slot[:, t, :], ties[:, t, :], ties[:, t, :], 0.0, ALU.add, ALU.bypass)
            fence()
            tt(slot, slot, n_above.unsqueeze(2).to_broadcast([P, NT, E]), ALU.add)
            fence()
            stt(mask, slot, float(TOP_K), ties, ALU.is_le, ALU.mult)
            fence()
            tt(mask, mask, above, ALU.add).then_inc(sem["mask_done"], 1)
            dve.wait_ge(sem["mask_done"], 1)
            dve.wait_ge(sem["exps_r"], 1)
            tt(wts, wts, mask, ALU.mult)
            fence()
            v.tensor_reduce(wsum, wts, X, ALU.add)
            fence()
            v.reciprocal(wsum, wsum)
            fence()
            tt(wts, wts, wsum.unsqueeze(2).to_broadcast([P, NT, E]), ALU.mult).then_inc(sem["weights_done"], 1)
            dve.wait_ge(sem["rank_mm"], 1)
            ranks = pb[7][:, 0:3 * E].rearrange("p (t e) -> p t e", e=E)
            stt(slot[:, 0:2, :], ranks[:, 0:2, :], 1000.0, mask[:, 0:2, :], ALU.add, ALU.mult)
            stt(slot[0:NS, 2, :], ranks[0:NS, 2, :], 1000.0, mask[0:NS, 2, :], ALU.add, ALU.mult)
            v.tensor_copy(counts, pb[7][:, 3 * E:4 * E])
            fence()
            ts(slot, slot, -1000.0, None, ALU.add)
            fence()
            slot_f = rt[:, 480:576]
            wts_f = rt[:, 384:480]

            def item(n):
                e = dve.value_load(items[0:1, bass.ds(n, 1), 0:1].rearrange("o a b -> o (a b)"),
                                   min_val=0, max_val=E - 1)
                c = dve.value_load(items[0:1, bass.ds(n, 1), 1:2].rearrange("o a b -> o (a b)"),
                                   min_val=0, max_val=5)
                return e, c

            def one_hot(out, e, c, weighted):
                for t, (r0, n) in enumerate(TILES):
                    places = iota_f[0:n, bass.ds(c * CAP, CAP)]
                    place = slot_f[0:n, bass.ds(e + t * E, 1)]
                    if weighted:
                        weight = wts_f[0:n, bass.ds(e + t * E, 1)]
                        last = ts(out[0:n, t, :].rearrange("p (a s) -> p a s", a=2),
                                  places.unsqueeze(1).to_broadcast([n, 2, CAP]), place, weight,
                                  ALU.is_equal, ALU.mult)
                    else:
                        last = ts(out[0:n, t, CAP:2 * CAP], places, place, None, ALU.is_equal)
                return last

            def split_low(place, i):
                p = pair_of(place)
                dve.wait_ge(hi_done[p], split(place, i))
                tt(w_lo[p][:, :], ring[:, 4 + slot_of(place), :], w_hi[p][:, :], ALU.subtract)\
                    .then_inc(lo_done[p], 1)

            def copy_gate_up(i, last_place):
                dve.wait_ge(pair_free[pair_of(last_place)], used(last_place, i))
                for b in (0, 1):
                    v.tensor_copy(gu_sb[:, b * 512:(b + 1) * 512], pb[b][:, :]).then_inc(sem["gu_copied"], 1)

            def gate_and_up(i, e):
                bias = [bias_gu[:, bass.ds(e * 16 + 8 * j, 8)].unsqueeze(2).to_broadcast([P, 8, CAP])
                        for j in range(2)]
                dve.wait_ge(sem["gu_turned"], i * 2)
                tt(g_buf, bank(4, KT), bias[0], ALU.add)
                tt(u_buf, bank(5, KT), bias[1], ALU.add)
                fence()
                ts(g_buf, g_buf, LIMIT, None, ALU.min).then_inc(sem["gate_ready"], 1)
                ts(u_buf, u_buf, LIMIT, -LIMIT, ALU.min, ALU.max)
                fence()
                stt(u_buf, u_buf, 1.0, g_buf, ALU.add, ALU.mult)
                fence()

            def activations(i):
                dve.wait_ge(sem["sigmoid_done"], i)
                tt(act_buf, u_buf, s_buf, ALU.mult)
                tt(act2[:, :, 0:CAP], u_buf, s_buf, ALU.mult)
                fence()
                tt(act2[:, :, CAP:2 * CAP], act_buf, act2[:, :, 0:CAP], ALU.subtract).then_inc(sem["act_ready"], 1)

            def scatter_columns(i, e, c):
                dve.wait_ge(sem["selw_turned"], i)
                one_hot(selw, e, c, True).then_inc(sem["selw_ready"], 1)

            def gather_columns(n):
                e, c = item(n)
                dve.wait_ge(sem["gather_mm"], n)
                one_hot(sel, e, c, False).then_inc(sem["sel_ready"], 1)

            def add_scattered(i, tiles):
                for k in tiles:
                    dve.wait_ge(sem["scatter_mm"], i * KT + (k + 1))
                    tt(accT[:, k, :], accT[:, k, :], pb[4 + k % 2][:, 0:TOK], ALU.add)\
                        .then_inc(sem["scatter_added"], 1)

            dve.wait_ge(sem["h_lo_done"], NT + 1)
            one_hot(sel, 0, 0, False).then_inc(sem["sel_ready"], 1)
            for c in range(4):
                ts(flags[:, c * E:(c + 1) * E], counts, float(CAP * (c + 1)), None, ALU.is_gt)
            fence()
            v.tensor_tensor_scan(prefix, flags, flags, 0.0, ALU.add, ALU.bypass)
            fence()
            ts(flags, prefix, kidx, None, ALU.is_le)
            fence()
            v.tensor_reduce(eidx[:, 0:1], flags, X, ALU.add)
            fence()
            ts(eidx[:, 1:2], eidx[:, 0:1], float(E), None, ALU.is_ge)
            for c in range(2, 5):
                fence()
                stt(eidx[:, 1:2], eidx[:, 0:1], float(E * c), eidx[:, 1:2], ALU.is_ge, ALU.add)
            fence()
            stt(eidx[:, 2:3], eidx[:, 1:2], -float(E), eidx[:, 0:1], ALU.mult, ALU.add)
            fence()
            v.tensor_copy(extra_items[:, 0:1], eidx[:, 2:3])
            ts(extra_items[:, 1:2], eidx[:, 1:2], 1.0, None, ALU.add)
            v.tensor_copy(n_extra_i[:, 0:1], prefix[0:1, 127:128])
            v.memset(n_extra_i[:, 1:2].bitcast(F32), 0.0)
            dve.drain().then_inc(sem["extras_made"], 1)
            dve.wait_ge(sem["hT_copied"], 2 * NT)
            for k in range(KT):
                dve.wait_ge(sem["bdown_mm"], k + 1)
                stt(accT[:, k, :], hT[:, k, :], ALPHA, pb[4 + k % 2][:, 0:TOK], ALU.mult, ALU.add)\
                    .then_inc(sem["acc_init"], 1)
            dve.wait_ge(sem["acc_init"], KT)
            dve.wait_ge(sem["conv_stored"], 16 * 3)
            v.memset(out_sb, 0.0)
            v.memset(selw, 0.0)
            dve.drain().then_inc(sem["selw_ready"], 1)
            dve.sem_inc(sem["out_copied"], 2)
            dve.wait_ge(sem["gather_mm"], 1)
            one_hot(sel, 1, 0, False).then_inc(sem["sel_ready"], 1)
            dve.wait_ge(sem["b_copied"], 1)
            split_low(7, 0)
            split_low(8, 0)
            split_low(10, 0)
            split_low(11, 0)
            dve.wait_ge(sem["items_ready"], 1)
            n_items = dve.value_load(items[0:1, LIST - 1, 0:1], min_val=0, max_val=N_EXTRA) + E
            copy_gate_up(0, PLACES - 1)
            with dve.Fori(1, n_items) as i:
                e, c = item(i - 1)
                for place in (0, 1, 2):
                    split_low(place, i)
                scatter_columns(i, e, c)
                gather_columns(i + 1)
                gate_and_up(i, e)
                split_low(4, i)
                activations(i)
                split_low(5, i)
                split_low(6, i)
                add_scattered(i - 1, range(0, 3))
                split_low(7, i)
                add_scattered(i - 1, range(3, 6))
                split_low(8, i)
                add_scattered(i - 1, range(6, KT))
                copy_gate_up(i, KT - 1)
                split_low(10, i)
                split_low(11, i)
            e, c = item(n_items - 1)
            for place in (0, 1, 2):
                split_low(place, n_items)
            gate_and_up(n_items, e)
            activations(n_items)
            scatter_columns(n_items, e, c)
            add_scattered(n_items - 1, range(KT))
            split_low(3, n_items)
            add_scattered(n_items, range(KT))
            fence()
            dve.wait_ge(sem["ln2_loaded"], 32)
            for t, (r0, n) in enumerate(TILES):
                dve.wait_ge(sem["y_turned"], t + 1)
                norm([pb[2 * t + half][0:n, :] for half in range(2)], n, y_nat[0:n, t, :], NT + t, "y_done")


_INS = ["x_prompt", "x_sample", "cache_k", "cache_v", "cache_logf", "state_conv", "page_table",
        "w_in", "b_forget", "conv_w", "conv_b", "conv_norm_g", "conv_norm_b",
        "w_attn_proj", "w_conv_proj", "w_out", "ln1_g", "ln1_b",
        "w_router", "b_router", "w_gate_up", "b_gate_up", "w_down", "b_down", "ln2_g", "ln2_b"]
_OUTS = [(1, 256, 1024), (8, 1, 1024), (1, 1, 256, 16, 64), (1, 1, 256, 16, 64), (1, 1, 256, 16),
         (1, 1, 30, 1024), (1, 8, 1, 16, 64), (1, 8, 1, 16, 64), (1, 8, 1, 16), (1, 8, 30, 1024)]


def kernel(**inputs):
    import numpy as np
    import concourse.bacc as bacc
    from concourse.bass_utils import run_bass_kernel_spmd

    nc = bacc.Bacc("TRN2", target_bir_lowering=False, num_devices=1)
    arrays, args = {}, []
    for name in _INS:
        a = np.ascontiguousarray(inputs[name])
        arrays[f"in_{name}"] = a
        args.append(nc.dram_tensor(f"in_{name}", a.shape, mybir.dt.from_np(a.dtype), kind="ExternalInput").ap())
    for i, shape in enumerate(_OUTS):
        args.append(nc.dram_tensor(f"out_{i}", shape, F32, kind="ExternalOutput").ap())
    trunk_step(nc, *args)
    r = run_bass_kernel_spmd(nc, [arrays], core_ids=[0])
    return tuple(r.results[0][f"out_{i}"] for i in range(len(_OUTS)))
```
